# Optimizing a Trainium2 kernel written in Bass

```python
import math
import jax, jax.numpy as jnp
from jax import lax
import numpy as np

D_MODEL = 2048
BATCH = 1
SEQ = 512
DEPTH = 1

CHUNK = 64
N_MEM = 256
RMS_EPS = 1e-5
NEG_INF = -1e30

A_HEAD_DIM = 64
A_WIDTH = D_MODEL // 4
A_HEADS = A_WIDTH // A_HEAD_DIM
A_PREV_CHUNKS = 8
A_MAX_REL = 128

B_HEAD_DIM = 64
B_WIDTH = D_MODEL // 2
B_HEADS = B_WIDTH // B_HEAD_DIM
B_LORA_W = 64
B_LORA_A = 64
B_LORA_V = 32
B_LORA_G = 160
B_GN_EPS = 64e-5

C_HEAD_DIM = 64
C_WIDTH = D_MODEL // 4
C_HEADS = C_WIDTH // C_HEAD_DIM
C_KV_HEADS = 2
C_KV_WIDTH = C_KV_HEADS * C_HEAD_DIM
C_WINDOW = 128
C_PREV_CHUNKS = C_WINDOW // CHUNK - 1

T5_BUCKETS = 32
T5_MAX_DIST = 128

MIX_WIDTH = A_WIDTH + B_WIDTH + C_WIDTH

X_HEADS = 4
X_HEAD_DIM = 128
X_WIDTH = X_HEADS * X_HEAD_DIM

D_FF = 4 * D_MODEL

B_SHIFT_SIZES = (B_WIDTH, B_WIDTH, B_WIDTH, B_LORA_W, B_LORA_A, B_LORA_G)
B_SHIFT_WIDTH = sum(B_SHIFT_SIZES)
B_SHIFT_SPLITS = [int(i) for i in np.cumsum(B_SHIFT_SIZES)[:-1]]
B_OFF = 3 * A_WIDTH
C_OFF = B_OFF + B_SHIFT_WIDTH
IN_BASE = C_OFF + C_WIDTH + 2 * C_KV_WIDTH

kernel_name = "hybrid_chunk_stream_encoder"

def rms_norm(x, g):
    x32 = x.astype(jnp.float32)
    y = x32 * lax.rsqrt(jnp.mean(x32 * x32, axis=-1, keepdims=True) + RMS_EPS)
    return y.astype(x.dtype) * g

def split_heads(t, n):
    return t.reshape(t.shape[:-1] + (n, t.shape[-1] // n))

def token_shift(p, mu):
    prev = jnp.pad(p, ((0, 0), (1, 0), (0, 0)))[:, :-1]
    return p + mu * (prev - p)

def chunk_band(t, n_prev):
    b, s, h, d = t.shape
    nc = s // CHUNK
    tc = jnp.pad(t.reshape(b, nc, CHUNK, h, d), ((0, 0), (n_prev, 0), (0, 0), (0, 0), (0, 0)))
    return jnp.concatenate([tc[:, j:j + nc] for j in range(n_prev + 1)], axis=2)

def band_valid(nc, n_prev):
    c = np.arange(nc)[:, None]
    j = np.repeat(np.arange(n_prev + 1), CHUNK)[None, :]
    return (c - n_prev + j) >= 0

def band_rel(n_prev):
    i = np.arange(CHUNK)[:, None]
    slot = np.arange((n_prev + 1) * CHUNK)[None, :]
    k_off = (slot // CHUNK - n_prev) * CHUNK + slot % CHUNK
    return i - k_off

def t5_bucket(rel):
    nb = T5_BUCKETS // 2
    max_exact = nb // 2
    ret = (rel > 0).astype(np.int32) * nb
    n = np.abs(rel)
    large = max_exact + (np.log(np.maximum(n, 1) / max_exact) / math.log(T5_MAX_DIST / max_exact) * (nb - max_exact)).astype(np.int32)
    large = np.minimum(large, nb - 1)
    return ret + np.where(n < max_exact, n, large)

def chunk_band_attention(q, k, v, rel_table):
    b, s, h, d = q.shape
    nc = s // CHUNK
    qc = q.reshape(b, nc, CHUNK, h, d)
    kb = chunk_band(k, A_PREV_CHUNKS)
    vb = chunk_band(v, A_PREV_CHUNKS)
    logits = jnp.einsum('bcqhd,bckhd->bchqk', qc, kb).astype(jnp.float32) * (d ** -0.5)
    rel_idx = np.clip(band_rel(A_PREV_CHUNKS), -A_MAX_REL, A_MAX_REL) + A_MAX_REL
    bias = jnp.transpose(rel_table[rel_idx], (2, 0, 1)).astype(jnp.float32)
    logits = logits + bias[None, None]
    valid = band_valid(nc, A_PREV_CHUNKS)
    logits = jnp.where(valid[None, :, None, None, :], logits, NEG_INF)
    p = jax.nn.softmax(logits, axis=-1).astype(v.dtype)
    o = jnp.einsum('bchqk,bckhd->bcqhd', p, vb)
    return o.reshape(b, s, h * d)

def sliding_sink_attention(q, k, v, sinks, t5_table):
    b, s, hq, d = q.shape
    hkv = k.shape[2]
    g = hq // hkv
    nc = s // CHUNK
    band = (C_PREV_CHUNKS + 1) * CHUNK
    qc = q.reshape(b, nc, CHUNK, hkv, g, d)
    kb = chunk_band(k, C_PREV_CHUNKS)
    vb = chunk_band(v, C_PREV_CHUNKS)
    logits = jnp.einsum('bcqkgd,bcskd->bckgqs', qc, kb).astype(jnp.float32) * (d ** -0.5)
    bucket = t5_bucket(-band_rel(C_PREV_CHUNKS))
    bias = jnp.transpose(t5_table[bucket], (2, 0, 1)).reshape(hkv, g, CHUNK, band).astype(jnp.float32)
    logits = logits + bias[None, None]
    valid = band_valid(nc, C_PREV_CHUNKS)
    logits = jnp.where(valid[None, :, None, None, None, :], logits, NEG_INF)
    sink = jnp.broadcast_to(sinks.astype(jnp.float32).reshape(hkv, g)[None, None, :, :, None, None], logits.shape[:-1] + (1,))
    p = jax.nn.softmax(jnp.concatenate([logits, sink], axis=-1), axis=-1)[..., :-1].astype(v.dtype)
    o = jnp.einsum('bckgqs,bcskd->bcqkgd', p, vb)
    return o.reshape(b, s, hq * d)

def wkv7_scan(r, w, k, v, a, bv):
    bsz, _, h, n = r.shape

    def step(state, inp):
        r_t, w_t, k_t, v_t, a_t, b_t = inp
        sa = jnp.einsum('bhij,bhj->bhi', state, a_t)
        state = state * w_t[:, :, None, :] + sa[..., None] * b_t[:, :, None, :] + v_t[..., None] * k_t[:, :, None, :]
        return state, jnp.einsum('bhij,bhj->bhi', state, r_t)

    xs = tuple(jnp.moveaxis(t.astype(jnp.float32), 1, 0) for t in (r, w, k, v, a, bv))
    _, ys = lax.scan(step, jnp.zeros((bsz, h, n, n), jnp.float32), xs)
    return jnp.moveaxis(ys, 0, 1)

def rwkv7_time_mix(pr, pk, pv, pw, pa, pg, vmix, w0, w_up, a0, a_up, g_up, k_k, k_a, r_k, ln_w, ln_b):
    b, s, c = pr.shape
    w_log = -jax.nn.softplus(-(w0 + jnp.tanh(pw) @ w_up)) - 0.5
    decay = jnp.exp(-jnp.exp(w_log.astype(jnp.float32)))
    v = pv
    if vmix is not None:
        v_first, pvl, v0, v_up = vmix
        v = pv + (v_first - pv) * jax.nn.sigmoid(v0 + pvl @ v_up)
    a = jax.nn.sigmoid(a0 + pa @ a_up)
    g = jax.nn.sigmoid(pg) @ g_up
    kk = split_heads((pk * k_k).astype(jnp.float32), B_HEADS)
    kk = kk / jnp.maximum(jnp.sqrt(jnp.sum(kk * kk, axis=-1, keepdims=True)), 1e-12)
    k = pk * (1.0 + (a - 1.0) * k_a)
    rh, kh, vh, ah = (split_heads(t, B_HEADS) for t in (pr, k, v, a))
    y = wkv7_scan(rh, split_heads(decay, B_HEADS), kh, vh, -kk, kk * ah.astype(jnp.float32))
    mean = jnp.mean(y, axis=-1, keepdims=True)
    var = jnp.mean(jnp.square(y - mean), axis=-1, keepdims=True)
    y = ((y - mean) * lax.rsqrt(var + B_GN_EPS)).reshape(b, s, c).astype(pr.dtype) * ln_w + ln_b
    bonus = jnp.sum(rh * kh * r_k, axis=-1, keepdims=True) * vh
    return (y + bonus.reshape(b, s, c)) * g, v

def setup_inputs(seed: int = 0) -> dict:
    key = jax.random.key(seed)
    ks = iter(jax.random.split(key, 40))
    nrm = lambda shape, scale: jax.random.normal(next(ks), shape, jnp.float32) * scale
    gain = lambda shape: 1.0 + nrm(shape, 0.01)
    uni = lambda shape: jax.random.uniform(next(ks), shape, jnp.float32, 0.05, 0.95)
    L = DEPTH
    w0_base = jnp.linspace(-6.0, -1.0, B_WIDTH, dtype=jnp.float32)
    return {
        "x": nrm((BATCH, SEQ, D_MODEL), 1.0),
        "mem": nrm((BATCH, N_MEM, D_MODEL), 1.0),
        "norm_mix": gain((L, D_MODEL)),
        "w_in": nrm((L, D_MODEL, IN_BASE), D_MODEL ** -0.5),
        "w_vres_down": nrm((L - 1, D_MODEL, B_LORA_V), D_MODEL ** -0.5),
        "w_out": nrm((L, MIX_WIDTH, D_MODEL), MIX_WIDTH ** -0.5),
        "a_rel_bias": nrm((L, 2 * A_MAX_REL + 1, A_HEADS), 0.1),
        "rwkv_mu": uni((L, B_SHIFT_WIDTH)),
        "rwkv_mu_vres": uni((L - 1, B_LORA_V)),
        "rwkv_w0": w0_base[None] + nrm((L, B_WIDTH), 0.1),
        "rwkv_w_up": nrm((L, B_LORA_W, B_WIDTH), 0.5 * B_LORA_W ** -0.5),
        "rwkv_a0": nrm((L, B_WIDTH), 0.1),
        "rwkv_a_up": nrm((L, B_LORA_A, B_WIDTH), B_LORA_A ** -0.5),
        "rwkv_v0": nrm((L - 1, B_WIDTH), 0.1),
        "rwkv_v_up": nrm((L - 1, B_LORA_V, B_WIDTH), B_LORA_V ** -0.5),
        "rwkv_g_up": nrm((L, B_LORA_G, B_WIDTH), B_LORA_G ** -0.5),
        "rwkv_k_k": 0.85 + nrm((L, B_WIDTH), 0.05),
        "rwkv_k_a": 1.0 + nrm((L, B_WIDTH), 0.05),
        "rwkv_r_k": nrm((L, B_HEADS, B_HEAD_DIM), 0.1),
        "rwkv_ln_w": gain((L, B_WIDTH)),
        "rwkv_ln_b": nrm((L, B_WIDTH), 0.01),
        "c_sinks": nrm((L, C_HEADS), 0.5),
        "t5_bias": nrm((T5_BUCKETS, C_HEADS), 0.1),
        "norm_x": gain((L, D_MODEL)),
        "norm_mem": gain((L, D_MODEL)),
        "x_wq": nrm((L, D_MODEL, X_WIDTH), D_MODEL ** -0.5),
        "x_wk": nrm((L, D_MODEL, X_WIDTH), D_MODEL ** -0.5),
        "x_wv": nrm((L, D_MODEL, X_WIDTH), D_MODEL ** -0.5),
        "x_wo": nrm((L, X_WIDTH, D_MODEL), X_WIDTH ** -0.5),
        "norm_mlp": gain((L, D_MODEL)),
        "mlp_w1": nrm((L, D_MODEL, D_FF), D_MODEL ** -0.5),
        "mlp_w2": nrm((L, D_FF, D_MODEL), D_FF ** -0.5),
        "norm_final": gain((D_MODEL,)),
    }

def reference(x, mem, norm_mix, w_in, w_vres_down, w_out, a_rel_bias, rwkv_mu, rwkv_mu_vres, rwkv_w0, rwkv_w_up, rwkv_a0, rwkv_a_up, rwkv_v0, rwkv_v_up, rwkv_g_up, rwkv_k_k, rwkv_k_a, rwkv_r_k, rwkv_ln_w, rwkv_ln_b, c_sinks, t5_bias, norm_x, norm_mem, x_wq, x_wk, x_wv, x_wo, norm_mlp, mlp_w1, mlp_w2, norm_final):
    b, s, _ = x.shape
    m = mem.shape[1]
    h = x
    v_first = None
    for l in range(DEPTH):
        xn = rms_norm(h, norm_mix[l])
        w_l = w_in[l] if l == 0 else jnp.concatenate([w_in[l], w_vres_down[l - 1]], axis=1)
        proj = xn @ w_l
        a_q, a_k, a_v = jnp.split(proj[..., :B_OFF], 3, axis=-1)
        b_cols = token_shift(proj[..., B_OFF:C_OFF], rwkv_mu[l])
        b_r, b_k, b_v, b_w, b_a, b_g = jnp.split(b_cols, B_SHIFT_SPLITS, axis=-1)
        c_q = proj[..., C_OFF:C_OFF + C_WIDTH]
        c_k = proj[..., C_OFF + C_WIDTH:C_OFF + C_WIDTH + C_KV_WIDTH]
        c_v = proj[..., C_OFF + C_WIDTH + C_KV_WIDTH:IN_BASE]
        if l == 0:
            vmix = None
        else:
            vmix = (v_first, token_shift(proj[..., IN_BASE:], rwkv_mu_vres[l - 1]), rwkv_v0[l - 1], rwkv_v_up[l - 1])

        y_a = chunk_band_attention(split_heads(a_q, A_HEADS), split_heads(a_k, A_HEADS), split_heads(a_v, A_HEADS), a_rel_bias[l])
        y_b, v_l = rwkv7_time_mix(b_r, b_k, b_v, b_w, b_a, b_g, vmix, rwkv_w0[l], rwkv_w_up[l], rwkv_a0[l], rwkv_a_up[l], rwkv_g_up[l], rwkv_k_k[l], rwkv_k_a[l], rwkv_r_k[l], rwkv_ln_w[l], rwkv_ln_b[l])
        if l == 0:
            v_first = v_l
        y_c = sliding_sink_attention(split_heads(c_q, C_HEADS), split_heads(c_k, C_KV_HEADS), split_heads(c_v, C_KV_HEADS), c_sinks[l], t5_bias)
        h = h + jnp.concatenate([y_a, y_b, y_c], axis=-1) @ w_out[l]

        xn = rms_norm(h, norm_x[l])
        mn = rms_norm(mem, norm_mem[l])
        q = (xn @ x_wq[l]).reshape(b, s, X_HEADS, X_HEAD_DIM)
        k = (mn @ x_wk[l]).reshape(b, m, X_HEADS, X_HEAD_DIM)
        v = (mn @ x_wv[l]).reshape(b, m, X_HEADS, X_HEAD_DIM)
        logits = jnp.einsum('bshd,bmhd->bhsm', q, k).astype(jnp.float32) * (X_HEAD_DIM ** -0.5)
        p = jax.nn.softmax(logits, axis=-1).astype(v.dtype)
        o = jnp.einsum('bhsm,bmhd->bshd', p, v).reshape(b, s, X_WIDTH)
        h = h + o @ x_wo[l]

        xn = rms_norm(h, norm_mlp[l])
        h = h + jnp.square(jax.nn.relu(xn @ mlp_w1[l])) @ mlp_w2[l]
    return rms_norm(h, norm_final)


_drawn_inputs = setup_inputs


def setup_inputs(seed=0):
    import zlib

    import numpy as np

    out = dict(_drawn_inputs(seed))
    spreads = {}
    factors = {'norm_mix': 7.124,
     'a_rel_bias': 27.993,
     'rwkv_w_up': 3.691,
     'rwkv_a0': 3.573,
     'rwkv_k_k': 30.472,
     'rwkv_ln_w': 64.0,
     'rwkv_ln_b': 64.0,
     'c_sinks': 8.0,
     't5_bias': 34.2,
     'norm_x': 28.959,
     'norm_mem': 29.241,
     'norm_mlp': 42.26,
     'norm_final': 30.309}
    for name, (base, spread) in spreads.items():
        noise = np.random.default_rng([zlib.crc32(name.encode()), seed]).standard_normal(out[name].shape)
        drawn = base * np.exp(spread * noise) if base else spread * noise
        out[name] = __import__('jax').numpy.asarray(drawn.astype(out[name].dtype))
    for name, factor in factors.items():
        out[name] = (out[name] * factor).astype(out[name].dtype)
    return out
```

```python
from contextlib import ExitStack

import numpy as np

import concourse.bass as bass
from concourse import mybir

F32 = mybir.dt.float32
F32R = mybir.dt.float32r
ALU = mybir.AluOpType
ACT = mybir.ActivationFunctionType
AX_X = mybir.AxisListType.X

P = 128
SEQ, D, N_MEM, D_FF = 512, 2048, 256, 8192
TT = SEQ // P
KT = D // P
L = 64
NC = SEQ // L
PAIRS = 8
A_TILES = 12
C_TILES = 6
QKV = A_TILES + C_TILES
UNITS = 8
RAW = 4
SPL = 2
LOOK = SPL - 1
LORA_W, PAIR_W, REST_W = 288, 384, 512
G_PAIR, G_QKV = 1, 1 + PAIRS
G_IN = G_QKV + QKV // 3
G_WOUT = G_IN
G_XK = G_WOUT + 4
G_XV, G_XQ, G_XO, G_MLP = G_XK + 1, G_XK + 2, G_XK + 3, G_XK + 4
MLP_CHUNKS = 8
G_ALL = G_MLP + 4 * MLP_CHUNKS
FT = D_FF // MLP_CHUNKS // P
RMS_EPS, GN_EPS = 1e-5, 64e-5
LOGW = float(np.exp(-0.5))
MASKED = -1e30
A_KEYS, C_KEYS = 512, 256
N_UNITS_ATT = 64
X_SCALE = 128.0 ** -0.5
MU_R, MU_K, MU_V, W0, A0, K_K, K_A, R_K, N_PRM = range(9)
NEG_W0, NEG_A0, ONE_MINUS_KA = range(3)
LEVELS = [2, 4, 8, 16, 32]


def hybrid_layer(nc, x, mem, gains, w_lora, w_pairs, w_rest, pair_prm, fin_prm, gup_tail, lora_mu,
                 a_line, c_line, sinks, norm_final, out):
    top = ExitStack()
    with top:
        def alloc(stack):
            return lambda name, shape, dt=F32: stack.enter_context(nc.sbuf_tensor(name, shape, dt))

        def sem(name):
            return top.enter_context(nc.semaphore(name))

        sb = alloc(top)
        act_hi = sb("act_hi", [P, KT, SEQ], F32R)
        act_lo = sb("act_lo", [P, KT, SEQ], F32R)
        w_raw = sb("w_raw", [P, RAW, 2 * REST_W])
        w_hi = sb("w_hi", [P, SPL, 2 * REST_W], F32R)
        w_lo = sb("w_lo", [P, SPL, 2 * REST_W], F32R)
        ident = sb("ident", [P, P])
        gain = sb("gain", [P, 4, KT])
        diag = sb("diag", [P, TT, P])
        ssq = sb("ssq", [P, 8])
        rms = sb("rms", [P, 8])
        ps = top.enter_context(nc.psum_tensor("ps", [P, 8, 512], F32))
        scr_y = nc.dram_tensor("scr_y", (PAIRS, P, SEQ), F32).ap()
        scr_qkv = nc.dram_tensor("scr_qkv", (QKV // 3, 3, P, SEQ), F32).ap()

        lay1, lay2, lay3 = ExitStack(), ExitStack(), ExitStack()
        s1 = alloc(lay1)
        x_mix = s1("x_mix", [P, TT, D])
        x_sq = s1("x_sq", [P, D])
        lay1.close()

        s2 = alloc(lay2)
        pad = [s2(f"pad{i}", [P, 1 + SEQ]) for i in range(3)]
        rr, kk_, vv = s2("r_s", [P, SEQ]), s2("k_s", [P, SEQ]), s2("v_s", [P, SEQ])
        sg, aa, cs = s2("sig_w", [P, SEQ]), s2("a_gate", [P, SEQ]), s2("cum_sig", [P, SEQ])
        g_pad = s2("g_pad", [P, NC, L + 1])
        g_inv = s2("g_inv", [P, SEQ])
        kkn, kp = s2("kk_norm", [P, SEQ]), s2("k_mod", [P, SEQ])
        m_ab, m_abT = s2("m_ab", [P, SEQ]), s2("m_abT", [P, SEQ])
        inv, t_lev = s2("inv", [P, SEQ]), s2("t_level", [P, SEQ])
        yb, yc, ysq, gs = s2("y_raw", [P, SEQ]), s2("y_cent", [P, SEQ]), s2("y_sq", [P, SEQ]), s2("gate", [P, SEQ])
        two = lambda name: [s2(f"{name}{i}", [P, SEQ]) for i in range(2)]
        rT, aT, b_tok, k_tok, v_tok = two("r_dec"), two("a_dec"), two("b_tok"), two("k_tok"), two("v_tok")
        makT, mrbT, mrkT, invT, bonv = two("makT"), two("mrbT"), two("mrkT"), two("invT"), two("bonus_v")
        g_last = s2("g_last", [P, 2, NC])
        z_s, u_s = s2("z_s", [P, L]), s2("u_s", [P, L])
        st_s, st_g = s2("state", [P, 2, L]), s2("state_decayed", [P, L])
        prm, prm2 = s2("prm", [P, N_PRM + P]), s2("prm2", [P, 3])
        fprm, gup2 = s2("fprm", [P, 2 + P]), s2("gup2", [P, P])
        lora = s2("lora", [P, 3, SEQ])
        lmu = s2("lora_mu", [P, 3])
        rm = s2("restart", [P, SEQ])
        eye2, ones2, mean2 = s2("eye2", [P, L]), s2("ones2", [P, P]), s2("mean2", [P, P])
        mk_up, mk_upi, mk_lo, mk_1, mk_1T = (s2(n, [P, L]) for n in ("mk_up", "mk_upi", "mk_lo", "mk_1", "mk_1T"))
        mk_lev = s2("mk_lev", [P, len(LEVELS), L])
        m128 = s2("m128", [P, 10, P])
        lay2.close()

        s3 = alloc(lay3)
        h = s3("h", [P, TT, D])
        mid_hi = s3("mid_hi", [P, FT, SEQ], F32R)
        mid_lo = s3("mid_lo", [P, FT, SEQ], F32R)
        x_tmp = ExitStack()
        s4 = alloc(x_tmp)
        qk = s4("qk", [P, 2, 2, SEQ])
        vt = s4("vt", [P, TT, 640])
        bias = s4("bias", [P, 2, A_KEYS])
        zeros = bias[:, 0, 0:N_MEM]
        att_s = s4("att_s", [P, 2, A_KEYS])
        att_p = s4("att_p", [P, 4, A_KEYS])
        att_pT = s4("att_pT", [P, 2, A_KEYS])
        att_c = s4("att_c", [P, 4, 4])
        sink = s4("sink", [P, 8])
        x_tmp.close()
        s5 = alloc(x_tmp)
        memx = s5("memx", [P, 2, D])
        x_tmp.close()
        s6 = alloc(lay3)
        xq_t, xk_t, xv_t = s6("xq_t", [P, 4, SEQ]), s6("xk_t", [P, 4, N_MEM]), s6("xv_t", [P, 4, N_MEM])
        xv_tok = s6("xv_tok", [P, 2, 512])
        x_zero = s6("x_zero", [P, N_MEM])
        x_s, x_p, x_pT = s6("x_s", [P, 2, N_MEM]), s6("x_p", [P, 4, N_MEM]), s6("x_pT", [P, 2, N_MEM])
        x_c = s6("x_c", [P, 4, 4])
        relu_t, sq_t = s6("relu_t", [P, 2, SEQ]), s6("sq_t", [P, 2, SEQ])
        gain_out = w_raw[:, 0:2, :].rearrange("p a b -> p (a b)")
        lay3.close()

        s = {n: sem(n) for n in """
            x_in gain_in line_in prm_in fprm_in lmu_in consts zeroed pool_step
            ssq_act ssq_dve ms_ready rms_sqrt diag_ready tr_mm norm_hi norm_lo
            w_hi_done w_split w_used in_done in_evac lora_shift lora_act
            small_prm shifted zw_mm za_mm zw_ev za_ev sq_k ss_mm ss_max ss_sqrt cum_ready g_ready e_ready bon_in bon_mm bon_ev
            vtok_mm vtok_ev ktok_mm ktok_ev btok_mm btok_ev ab_ready kt_ready bt_ready
            mak_mm mak_ev mrk_mm mrk_ev mrb_mm mrb_ev mab_mm mabT_mm mab_ev mabT_ev inv_init
            t_mm t_ev x_mm x_ev xT_mm xT_ev
            z_mm z_ev u_mm u_ev s_mm s_ev y_mm y_ev mean_mm yc_ready ysq_ready var_mm var_eps var_sqrt gate_mm gate_ev y_fin y_stored
            qkv_stored vy_in y_hi y_lo vt_mm vt_ev qk_in bias_in bias_ready sink_in
            sc_mm sc_max sc_neg p_exp p_ready pT_mm pT_ev o_mm o_hi o_lo
            h_in mem_in gout_in bank_done bank_evac xs_mm xs_max xs_neg xp_exp xp_ready xpT_mm xpT_ev xo_mm xo_hi xo_lo xvt_mm xvt_ev
            relu_done mid_hi_done mid_done out_ready out_stored
            """.split()}
        w_landed = [sem(f"w_landed{i}") for i in range(RAW)]

        def part(c):
            return slice(c * L, (c + 1) * L)

        HALF = (slice(0, L), slice(L, P))

        def chunks(buf):
            return buf[:, :].rearrange("p (c t) -> p c t", c=NC)

        def bank(b):
            return ps[:, b, :]

        def falling(v):
            return v[:, ::-1]

        def over_chunks(m):
            return m.rearrange("p (o t) -> p o t", o=1).to_broadcast([P, NC, L])

        def col(buf, i):
            return buf[:, i:i + 1]

        def width_of(kind):
            return 2 * {"lora": LORA_W, "pair": PAIR_W, "rest": REST_W}[kind]

        S_WOUT, S_XK, S_XV, S_XQ, S_XO, S_MLP = 0, 4, 5, 6, 7, 11

        def a_window(i):
            return 0, P * (i + 1)

        def c_window(i):
            return (0, P) if i == 0 else (P * (i - 1), 2 * P)

        def unit_of(n):
            t, half, i = n // 8, (n // 4) % 2, n % 4
            return (("A", t, half, i) + a_window(i)) if n < 32 else (("C", t, half, i) + c_window(i))

        block = top.enter_context(nc.Block())

        @block.sync
        def _(sp):
            def unit(n_wait, slot, use, dst_w, src):
                if n_wait is not None:
                    sp.wait_ge(s["w_split"], n_wait)
                sp.dma_start(w_raw[:, slot, 0:dst_w], src).then_inc(w_landed[slot], 16)

            for t in range(TT):
                sp.dma_start(x_mix[:, t, :], x[t * P:(t + 1) * P, :]).then_inc(s["x_in"], 16)
            for u in range(UNITS):
                unit(u - RAW + 1 if u >= RAW else None, u % RAW, None, width_of("lora"), w_lora[u])
            with sp.Fori(0, G_IN - 1) as j:
                for u in range(UNITS):
                    unit(UNITS * (j + 1) + u - RAW + 1, u % RAW, None, width_of("pair"),
                         w_pairs[bass.ds(UNITS * j + u, 1)].rearrange("o p n -> p (o n)"))
            with sp.Fori(0, G_ALL - G_IN) as j:
                for u in range(UNITS):
                    unit(UNITS * (j + G_IN) + u - RAW + 1, u % RAW, None, width_of("rest"),
                         w_rest[bass.ds(UNITS * j + u, 1)].rearrange("o p n -> p (o n)"))
            for t in range(TT):
                sp.wait_ge(s["out_ready"], t + 1)
                sp.dma_start(out[t * P:(t + 1) * P, :], h[:, t, :]).then_inc(s["out_stored"], 16)
            sp.wait_ge(s["out_stored"], 16 * TT)

        @block.gpsimd
        def _(pool):
            steps = [0]

            def step(ins):
                steps[0] += 1
                ins.then_inc(s["pool_step"], 1)
                pool.wait_ge(s["pool_step"], steps[0])

            pool.dma_start(gain[:, :, :], gains).then_inc(s["gain_in"], 16)
            step(nc.gpsimd.memset(ident[:, :], 0.0))
            step(nc.gpsimd.affine_select(out=ident[:, :], in_=ident[:, :], compare_op=ALU.not_equal, fill=1.0,
                                         base=0, pattern=[[-1, P]], channel_multiplier=1))
            pool.sem_inc(s["zeroed"], 1)
            pool.wait_ge(s["tr_mm"], KT)
            pool.dma_start(prm[:, :], pair_prm[0]).then_inc(s["prm_in"], 16)
            pool.dma_start(fprm[:, :], fin_prm[0]).then_inc(s["fprm_in"], 16)
            pool.dma_start(gup2[96:P, :], gup_tail[0]).then_inc(s["fprm_in"], 16)
            pool.dma_start(lmu[:, :], lora_mu).then_inc(s["lmu_in"], 16)
            for i, (cmp, base) in enumerate(((ALU.is_gt, 0), (ALU.is_ge, 0))):
                step(nc.gpsimd.memset(m128[:, i, :], 1.0))
                step(nc.gpsimd.affine_select(out=m128[:, i, :], in_=m128[:, i, :], compare_op=cmp, fill=0.0,
                                             base=base, pattern=[[1, P]], channel_multiplier=-1))
            step(nc.gpsimd.memset(m128[:, 2, :], 1.0))
            step(nc.gpsimd.affine_select(out=m128[:, 2, :], in_=m128[:, 2, :], compare_op=ALU.is_gt, fill=0.0,
                                         base=0, pattern=[[-1, P]], channel_multiplier=1))
            def level(dst, b, transposed):
                step(nc.gpsimd.memset(dst, 0.0))
                v = dst.rearrange("p (n t) -> p n t", t=2 * b)
                step(nc.gpsimd.memset(v[:, :, b:2 * b] if transposed else v[:, :, 0:b], 1.0))
                lo, hi = (0, b - 1) if transposed else (b, 2 * b - 1)
                step(nc.gpsimd.affine_select(out=v, in_=v, compare_op=ALU.is_ge, fill=0.0, base=-lo,
                                             pattern=[[-2 * b, P // (2 * b)], [0, 2 * b]], channel_multiplier=1))
                step(nc.gpsimd.affine_select(out=v, in_=v, compare_op=ALU.is_ge, fill=0.0, base=hi,
                                             pattern=[[2 * b, P // (2 * b)], [0, 2 * b]], channel_multiplier=-1))
            level(m128[:, 3, :], 1, False)
            level(m128[:, 4, :], 1, True)
            for i, b in enumerate(LEVELS):
                level(m128[:, 5 + i, :], b, False)
            for dst, src in ((mk_up, 0), (mk_upi, 1), (mk_lo, 2), (mk_1, 3), (mk_1T, 4)):
                for hf in HALF:
                    step(nc.gpsimd.tensor_copy(dst[hf, :], m128[hf, src, hf]))
            for i in range(len(LEVELS)):
                for hf in HALF:
                    step(nc.gpsimd.tensor_copy(mk_lev[hf, i, :], m128[hf, 5 + i, hf]))
            for hf in HALF:
                step(nc.gpsimd.tensor_copy(eye2[hf, :], ident[hf, hf]))
            step(nc.gpsimd.memset(ones2[:, :], 0.0))
            step(nc.gpsimd.memset(mean2[:, :], 0.0))
            for hf in HALF:
                step(nc.gpsimd.memset(ones2[hf, hf], 1.0))
                step(nc.gpsimd.memset(mean2[hf, hf], 1.0 / L))
            step(nc.gpsimd.memset(rm[:, :], 1.0))
            step(nc.gpsimd.memset(chunks(rm)[:, :, 0:1], 0.0))
            for i in range(3):
                step(nc.gpsimd.memset(pad[i][:, 0:1], 0.0))
            step(nc.gpsimd.memset(g_pad[:, :, 0:1], 1.0))
            pool.sem_inc(s["consts"], 1)
            for g in range(G_PAIR, G_IN):
                q = g - 2
                if 0 <= q < PAIRS - 1:
                    pool.wait_ge(s["bon_ev"], q + 1)
                    pool.dma_start(prm[:, :], pair_prm[q + 1]).then_inc(s["prm_in"], 16)
                f = g - 4
                if 0 <= f < PAIRS:
                    pool.wait_ge(s["y_fin"], f + 1)
                    pool.dma_start(scr_y[f], yc[:, :]).then_inc(s["y_stored"], 16)
                    if f < PAIRS - 1:
                        pool.dma_start(fprm[:, :], fin_prm[f + 1]).then_inc(s["fprm_in"], 16)
                        pool.dma_start(gup2[96:P, :], gup_tail[f + 1]).then_inc(s["fprm_in"], 16)
                b = g - G_QKV
                if b >= 0:
                    pool.wait_ge(s["in_evac"], 3 * (g + 1))
                    for m in range(3):
                        pool.dma_start(scr_qkv[b, m], pad[m][:, 1:1 + SEQ]).then_inc(s["qkv_stored"], 16)
            pool.wait_ge(s["qkv_stored"], 48 * (QKV // 3))
            pool.wait_ge(s["y_stored"], 16 * PAIRS)
            hv = h[:, :, :].rearrange("p t (q n) -> p (t q) n", n=SEQ)
            for i, t in enumerate((8, 9, 10, 11, 17)):
                pool.dma_start(hv[:, i, :], scr_qkv[t // 3, t % 3]).then_inc(s["vy_in"], 16)
            for f in range(PAIRS):
                pool.dma_start(hv[:, 8 + f, :], scr_y[f]).then_inc(s["vy_in"], 16)
            pool.dma_start(sink[:, :], sinks.to_broadcast([P, 8])).then_inc(s["sink_in"], 16)
            for t in range(8):
                qt, kt = (t, 4 + t) if t < 4 else (A_TILES + t - 4, A_TILES + 4)
                if t >= 2:
                    pool.wait_ge(s["sc_mm"], 8 * (t - 1))
                pool.dma_start(qk[:, t % 2, 0, :], scr_qkv[qt // 3, qt % 3]).then_inc(s["qk_in"], 16)
                pool.dma_start(qk[:, t % 2, 1, :], scr_qkv[kt // 3, kt % 3]).then_inc(s["qk_in"], 16)
                for half in range(2):
                    n = 2 * t + half
                    line, w = (a_line, A_KEYS) if t < 4 else (c_line, C_KEYS)
                    head = n if t < 4 else (t - 4) + 4 * half
                    if n >= 2:
                        pool.wait_ge(s["sc_max"], 4 * (n - 1))
                    hankel = bass.AP(line.tensor, line[head, 0:1].offset, [[1, P], [1, w]])
                    pool.dma_start(bias[:, n % 2, 0:w], hankel).then_inc(s["bias_in"], 16)
                    pool.wait_ge(s["bias_in"], 16 * (n + 1))
                    step(nc.gpsimd.memset(bias[0:L, n % 2, 0:L], MASKED))
                    if t >= 4:
                        step(nc.gpsimd.memset(bias[0:L, n % 2, w - L:w], MASKED))
                        step(nc.gpsimd.memset(bias[L:P, n % 2, P:w], MASKED))
                    pool.sem_inc(s["bias_ready"], 1)
            pool.wait_ge(s["y_lo"], 1)
            pool.wait_ge(s["vt_mm"], TT)
            for t in range(TT):
                pool.dma_start(h[:, t, :], x[t * P:(t + 1) * P, :]).then_inc(s["h_in"], 16)
            pool.wait_ge(s["o_lo"], 8)
            for t in range(2):
                pool.dma_start(memx[:, t, :], mem[t * P:(t + 1) * P, :]).then_inc(s["mem_in"], 16)
            pool.wait_ge(s["tr_mm"], 2 * KT)
            nc.gpsimd.memset(x_zero[:, :], 0.0).then_inc(s["zeroed"], 1)
            pool.wait_ge(s["w_split"], UNITS * G_ALL)
            pool.dma_start(gain_out, norm_final.to_broadcast([P, D])).then_inc(s["gout_in"], 16)

        @block.scalar
        def _(act):
            def copy(dst, src, scale=1.0):
                return nc.scalar.activation(dst, src, ACT.Copy, scale=scale)

            def hi(n, slot, landed, dst_slot, w, free=True):
                act.wait_ge(w_landed[slot], 16 * landed)
                if free:
                    act.wait_ge(s["w_used"], n - SPL + 1)
                copy(w_hi[:, dst_slot, 0:w], w_raw[:, slot, 0:w]).then_inc(s["w_hi_done"], 1)

            def hi_next(g, u, w, w_next):
                v = u + LOOK
                gg, v, ww = (g, v, w) if v < UNITS else (g + 1, v - UNITS, w_next)
                if ww is not None:
                    hi(UNITS * gg + v, v % RAW, 2 * gg + v // RAW + 1, v % SPL, ww, True)

            def norm(k, src, tiles, gidx, dst, n):
                for t in range(tiles // 2):
                    nc.scalar.activation(ps[:, 0:4, :].rearrange("p a b -> p (a b)"), src[:, t, :], ACT.Square,
                                         accum_out=ssq[:, t:t + 1])
                    act.drain()
                act.sem_inc(s["ssq_act"], 1)
                act.wait_ge(s["ms_ready"], k + 1)
                nc.scalar.activation(rms[:, 4:4 + tiles], rms[:, 0:tiles], ACT.Sqrt).then_inc(s["rms_sqrt"], 1)
                if dst is None:
                    return
                for kt in range(KT):
                    act.wait_ge(s["tr_mm"], KT * k + kt + 1)
                    copy(dst[:, kt, :], ps[:, kt % 8, 0:n], scale=gain[:, gidx, kt:kt + 1]).then_inc(s["norm_hi"], 1)

            act.wait_ge(s["x_in"], 16 * TT)
            act.wait_ge(s["gain_in"], 16)
            norm(0, x_mix, TT, 0, act_hi, SEQ)
            for v in range(LOOK):
                hi(v, v, 1, v, width_of("lora"), False)

            def gap(e, g):
                q, f = g - 2, g - 4
                elem, fin = 0 <= q < PAIRS, 0 <= f < PAIRS
                par = q % 2
                if e == 0 and elem:
                    act.wait_ge(s["small_prm"], q + 1)
                    act.wait_ge(s["zw_mm"], q + 1)
                    nc.scalar.activation(sg[:, :], bank(4), ACT.Exp, scale=-1.0,
                                         bias=col(prm2, NEG_W0)).then_inc(s["zw_ev"], 1)
                    act.wait_ge(s["za_mm"], q + 1)
                    nc.scalar.activation(aa[:, :], bank(5), ACT.Exp, scale=-1.0,
                                         bias=col(prm2, NEG_A0)).then_inc(s["za_ev"], 1)
                    act.wait_ge(s["shifted"], q + 1)
                    nc.scalar.activation(pad[0][:, 1:1 + SEQ], kk_[:, :], ACT.Square,
                                         scale=col(prm, K_K)).then_inc(s["sq_k"], 1)
                if e == 0 and fin:
                    act.wait_ge(s["yc_ready"], f + 1)
                    nc.scalar.activation(ysq[:, :], yc[:, :], ACT.Square).then_inc(s["ysq_ready"], 1)
                if e == 1 and elem:
                    act.wait_ge(s["vtok_mm"], q + 1)
                    copy(v_tok[par][:, :], bank(3)).then_inc(s["vtok_ev"], 1)
                if e == 2 and elem:
                    act.wait_ge(s["ss_max"], q + 1)
                    nc.scalar.activation(pad[1][:, 1:1 + SEQ], pad[1][:, 1:1 + SEQ], ACT.Sqrt).then_inc(s["ss_sqrt"], 1)
                if e == 2 and fin:
                    act.wait_ge(s["var_eps"], f + 1)
                    nc.scalar.activation(ysq[:, :], ysq[:, :], ACT.Sqrt).then_inc(s["var_sqrt"], 1)
                if e == 2 and elem:
                    act.wait_ge(s["cum_ready"], q + 1)
                    nc.scalar.activation(g_pad[:, :, 1:1 + L], chunks(cs), ACT.Exp, scale=-LOGW).then_inc(s["g_ready"], 1)
                    nc.scalar.activation(g_inv[:, :], cs[:, :], ACT.Exp, scale=LOGW).then_inc(s["g_ready"], 1)
                if e == 2 and fin:
                    act.wait_ge(s["gate_mm"], f + 1)
                    copy(gs[:, :], bank(5)).then_inc(s["gate_ev"], 1)
                if e == 4 and elem:
                    act.wait_ge(s["ktok_mm"], q + 1)
                    copy(k_tok[par][:, :], bank(3)).then_inc(s["ktok_ev"], 1)
                if e == 5 and elem:
                    act.wait_ge(s["btok_mm"], q + 1)
                    copy(b_tok[par][:, :], bank(3)).then_inc(s["btok_ev"], 1)

            for g in range(G_IN):
                c, f = g - 3, g - 4
                chain = 0 <= c < PAIRS
                w = width_of("lora" if g == 0 else "pair")
                w_next = width_of("pair" if g + 1 < G_IN else "rest")
                if 0 <= f < PAIRS:
                    act.wait_ge(s["y_mm"], f + 1)
                    copy(yb[:, :], bank(7)).then_inc(s["y_ev"], 1)
                for u in range(UNITS):
                    hi_next(g, u, w, w_next)
                    if g == 1 and u == 0:
                        act.wait_ge(s["lora_shift"], 1)
                        nc.scalar.activation(lora[0:L, 0, :], lora[0:L, 0, :], ACT.Tanh).then_inc(s["lora_act"], 1)
                        nc.scalar.activation(lora[:, 1:3, :], lora[:, 1:3, :], ACT.Exp, scale=-1.0).then_inc(s["lora_act"], 1)
                    if chain:
                        act.wait_ge(s["z_mm"], NC * c + u + 1)
                        copy(z_s[:, :], ps[:, 6, 0:L]).then_inc(s["z_ev"], 1)
                    gap(2 * u, g)
                    if chain:
                        act.wait_ge(s["u_mm"], NC * c + u + 1)
                        copy(u_s[:, :], ps[:, 6, L:2 * L]).then_inc(s["u_ev"], 1)
                    gap(2 * u + 1, g)
                if g == 1:
                    act.wait_ge(s["lora_shift"], 1)
                if 2 <= g < G_QKV + 1:
                    act.wait_ge(s["bon_ev"], g - 1)
                if g > G_QKV:
                    act.wait_ge(s["qkv_stored"], 48 * (g - G_QKV))
                if g == 0:
                    act.wait_ge(s["consts"], 1)
                for m in range(3):
                    tile = 3 * (g - G_QKV) + m
                    is_q = g >= G_QKV and (tile < 4 or A_TILES <= tile < A_TILES + 4)
                    act.wait_ge(s["in_done"], 3 * g + m + 1)
                    copy(pad[m][:, 1:1 + SEQ], bank(m), scale=0.125 if is_q else 1.0).then_inc(s["in_evac"], 1)

            hv = h[:, :, :].rearrange("p t (q n) -> p (t q) n", n=SEQ)
            act.wait_ge(s["vy_in"], 16 * 13)
            copy(act_hi[:, 4:4 + PAIRS, :], hv[:, 8:8 + PAIRS, :]).then_inc(s["y_hi"], 1)
            for kb in range(TT):
                act.wait_ge(s["vt_mm"], kb + 1)
                copy(vt[:, kb, :], ps[:, 6:8, :].rearrange("p a b -> p (a b)")[:, 0:640]).then_inc(s["vt_ev"], 1)
            act.wait_ge(s["sink_in"], 16)
            for st in range(N_UNITS_ATT + 3):
                n = st
                if n < N_UNITS_ATT:
                    kind, t, half, i, key0, keys = unit_of(n)
                    act.wait_ge(s["sc_neg"], n + 1)
                    if n >= 4:
                        act.wait_ge(s["pT_mm"], n - 3)
                    if kind == "C":
                        head = (t - 4) + 4 * half
                        nc.scalar.activation(att_c[:, n % 4, 3:4], sink[:, head:head + 1], ACT.Exp,
                                             bias=att_c[:, n % 4, 1:2])
                    nc.scalar.activation(att_p[:, n % 4, 0:keys], att_s[:, n % 2, 0:keys], ACT.Exp,
                                         bias=att_c[:, n % 4, 1:2],
                                         accum_out=att_c[:, n % 4, 2:3]).then_inc(s["p_exp"], 1)
                n = st - 2
                if 0 <= n < N_UNITS_ATT:
                    keys = unit_of(n)[5]
                    act.wait_ge(s["pT_mm"], n + 1)
                    if n >= 2:
                        act.wait_ge(s["o_mm"], n - 1)
                    copy(att_pT[:, n % 2, 0:keys], ps[:, 2 + n % 2, 0:keys]).then_inc(s["pT_ev"], 1)
                n = st - 3
                if n >= 0 and n % 8 == 7:
                    t = n // 8
                    act.wait_ge(s["o_mm"], n + 1)
                    copy(act_hi[:, t if t < 4 else t + 8, :], bank(4 + t % 2)).then_inc(s["o_hi"], 1)

            for g in range(G_WOUT, G_XK):
                for u in range(UNITS):
                    hi_next(g, u, width_of("rest"), width_of("rest"))
            act.wait_ge(s["mem_in"], 32)
            act.wait_ge(s["bank_evac"], 4 * S_XK)
            mem_hi = mid_hi[:, :, :].rearrange("p a (b n) -> p (a b) n", n=N_MEM)
            norm(1, memx, 2, 2, mem_hi, N_MEM)
            for g in (G_XK, G_XV):
                for u in range(UNITS):
                    hi_next(g, u, width_of("rest"), width_of("rest"))
            act.wait_ge(s["bank_evac"], 4 * S_XQ)
            norm(2, h, TT, 1, act_hi, SEQ)
            for u in range(UNITS):
                hi_next(G_XQ, u, width_of("rest"), width_of("rest"))
            for kb in range(2):
                act.wait_ge(s["xvt_mm"], kb + 1)
                copy(xv_tok[:, kb, :], bank(6)).then_inc(s["xvt_ev"], 1)
            for st in range(16 + 3):
                n = st
                if n < 16:
                    act.wait_ge(s["xs_neg"], n + 1)
                    if n >= 4:
                        act.wait_ge(s["xpT_mm"], n - 3)
                    nc.scalar.activation(x_p[:, n % 4, :], x_s[:, n % 2, :], ACT.Exp, bias=x_c[:, n % 4, 1:2],
                                         accum_out=x_c[:, n % 4, 2:3]).then_inc(s["xp_exp"], 1)
                n = st - 2
                if 0 <= n < 16:
                    act.wait_ge(s["xpT_mm"], n + 1)
                    if n >= 2:
                        act.wait_ge(s["xo_mm"], n - 1)
                    copy(x_pT[:, n % 2, :], ps[:, 2 + n % 2, 0:N_MEM]).then_inc(s["xpT_ev"], 1)
                n = st - 3
                if n >= 0 and n % 4 == 3:
                    act.wait_ge(s["xo_mm"], n + 1)
                    copy(mid_hi[:, n // 4, :], bank(4 + (n // 4) % 2)).then_inc(s["xo_hi"], 1)
            for u in range(UNITS):
                hi_next(G_XO, u, width_of("rest"), width_of("rest"))
            act.wait_ge(s["bank_evac"], 4 * S_MLP)
            norm(3, h, TT, 3, act_hi, SEQ)

            def relu_tiles(c, j, tiles):
                for m in tiles:
                    r = m % 2
                    act.wait_ge(s["bank_done"], 4 * (S_MLP + 6 * c + j) + m + 1)
                    if m >= 2:
                        act.wait_ge(s["bank_evac"], 4 * (S_MLP + 6 * c + j) + m - 1)
                    nc.scalar.activation(relu_t[:, r, :], bank(4 * ((S_MLP + j) % 2) + m), ACT.Relu).then_inc(s["relu_done"], 1)
                    act.wait_ge(s["relu_done"], 8 * c + 4 * j + m + 1)
                    nc.scalar.activation(mid_hi[:, 4 * j + m, :], relu_t[:, r, :], ACT.Square).then_inc(s["mid_hi_done"], 1)

            def mlp_chunk(c, last):
                g0 = G_MLP + 4 * c
                for b in range(4):
                    for u in range(UNITS):
                        if b in (1, 2) and u == 0:
                            relu_tiles(c, b - 1, (2, 3))
                        hi_next(g0 + b, u, width_of("rest"), None if last and b == 3 else width_of("rest"))
                        if b < 2 and u == UNITS - 1:
                            relu_tiles(c, b, (0, 1))

            with act.Fori(0, MLP_CHUNKS - 1) as c:
                mlp_chunk(c, False)
            mlp_chunk(MLP_CHUNKS - 1, True)
            act.wait_ge(s["bank_evac"], 4 * (S_MLP + 6 * MLP_CHUNKS))
            norm(4, h, TT, None, None, SEQ)

        @block.vector
        def _(dve):
            V = nc.vector

            def lo_next(g, u, w, w_next):
                v = u + LOOK
                gg, v, ww = (g, v, w) if v < UNITS else (g + 1, v - UNITS, w_next)
                if ww is not None:
                    lo(UNITS * gg + v, v % RAW, v % SPL, ww)

            def lo(n, slot, dst_slot, w):
                dve.wait_ge(s["w_hi_done"], n + 1)
                V.tensor_tensor(w_lo[:, dst_slot, 0:w], w_raw[:, slot, 0:w], w_hi[:, dst_slot, 0:w].bitcast(F32),
                                ALU.subtract).then_inc(s["w_split"], 1)

            def norm(k, src, tiles, gidx, dst_hi, dst_lo, n):
                for t in range(tiles // 2, tiles):
                    V.tensor_tensor_reduce(out=ps[:, 4:8, :].rearrange("p a b -> p (a b)"), in0=src[:, t, :],
                                           in1=src[:, t, :], scale=1.0, scalar=0.0, op0=ALU.mult, op1=ALU.add,
                                           accum_out=ssq[:, t:t + 1])
                    dve.drain()
                dve.wait_ge(s["ssq_act"], k + 1)
                V.tensor_scalar(rms[:, 0:tiles], ssq[:, 0:tiles], 1.0 / D, RMS_EPS, ALU.mult, ALU.add).then_inc(s["ms_ready"], 1)
                dve.wait_ge(s["rms_sqrt"], k + 1)
                V.reciprocal(rms[:, 0:tiles], rms[:, 4:4 + tiles])
                dve.drain()
                if dst_hi is None:
                    return
                for t in range(tiles):
                    V.tensor_scalar(diag[:, t, :], ident[:, :], rms[:, t:t + 1], None, ALU.mult).then_inc(s["diag_ready"], 1)
                for kt in range(KT):
                    dve.wait_ge(s["norm_hi"], KT * k + kt + 1)
                    V.scalar_tensor_tensor(dst_lo[:, kt, :], ps[:, kt % 8, 0:n], gain[:, gidx, kt:kt + 1],
                                           dst_hi[:, kt, :].bitcast(F32), ALU.mult, ALU.subtract).then_inc(s["norm_lo"], 1)

            dve.wait_ge(s["x_in"], 16 * TT)
            dve.wait_ge(s["gain_in"], 16)
            dve.wait_ge(s["zeroed"], 1)
            norm(0, x_mix, TT, 0, act_hi, act_lo, SEQ)
            for v in range(LOOK):
                lo(v, v, v, width_of("lora"))
            T1, T2 = pad[0][:, 1:1 + SEQ], pad[1][:, 1:1 + SEQ]
            ka_col, rk_col, kk_col = col(prm, K_A), col(prm, R_K), col(prm, K_K)

            def masked(dst, b, m):
                return V.tensor_tensor(chunks(dst), ps[:, b, :].rearrange("p (c t) -> p c t", c=NC),
                                       over_chunks(m), ALU.mult)

            def gap(e, g):
                q, f = g - 2, g - 4
                elem, fin = 0 <= q < PAIRS, 0 <= f < PAIRS
                par = q % 2
                if e == 0 and elem:
                    dve.wait_ge(s["prm_in"], 16 * (q + 1))
                    V.tensor_scalar(prm2[:, 0:2], prm[:, W0:W0 + 2], -1.0, None, ALU.mult)
                    V.tensor_scalar(prm2[:, 2:3], ka_col, -1.0, 1.0, ALU.mult, ALU.add)
                    dve.drain()
                    dve.sem_inc(s["small_prm"], 1)
                    dve.wait_ge(s["in_evac"], 3 * (q + 2))
                    for dst, p in zip((rr, kk_, vv), pad):
                        V.tensor_tensor(dst[:, :], p[:, 0:SEQ], p[:, 1:1 + SEQ], ALU.subtract)
                    dve.drain()
                    for i, (dst, p) in enumerate(zip((rr, kk_, vv), pad)):
                        last = V.scalar_tensor_tensor(dst[:, :], dst[:, :], col(prm, MU_R + i), p[:, 1:1 + SEQ],
                                                      ALU.mult, ALU.add)
                    last.then_inc(s["shifted"], 1)
                if e == 0 and fin:
                    dve.wait_ge(s["mean_mm"], f + 1)
                    if f:
                        dve.wait_ge(s["y_stored"], 16 * f)
                    V.tensor_tensor(yc[:, :], yb[:, :], bank(3), ALU.subtract).then_inc(s["yc_ready"], 1)
                if e == 1 and elem:
                    dve.wait_ge(s["zw_ev"], q + 1)
                    dve.wait_ge(s["za_ev"], q + 1)
                    V.tensor_scalar(sg[:, :], sg[:, :], 1.0, None, ALU.add)
                    V.tensor_scalar(aa[:, :], aa[:, :], 1.0, None, ALU.add)
                    dve.drain()
                    V.reciprocal(sg[:, :], sg[:, :])
                    V.reciprocal(aa[:, :], aa[:, :])
                    dve.drain()
                    V.tensor_tensor_scan(cs[:, :], rm[:, :], sg[:, :], 0.0, ALU.mult, ALU.add).then_inc(s["cum_ready"], 1)
                    V.tensor_scalar(kp[:, :], aa[:, :], ka_col, prm2[:, 2:3], ALU.mult, ALU.add)
                    dve.wait_ge(s["ss_mm"], q + 1)
                    V.tensor_scalar(T2, bank(4), 1e-24, None, ALU.max).then_inc(s["ss_max"], 1)
                if e == 2 and fin:
                    dve.wait_ge(s["var_mm"], f + 1)
                    V.tensor_scalar(ysq[:, :], bank(3), GN_EPS, None, ALU.add).then_inc(s["var_eps"], 1)
                if e == 2 and elem:
                    dve.drain()
                    V.tensor_tensor(kp[:, :], kp[:, :], kk_[:, :], ALU.mult)
                    dve.drain()
                    V.scalar_tensor_tensor(T1, rr[:, :], rk_col, kp[:, :], ALU.mult, ALU.mult).then_inc(s["bon_in"], 1)
                    dve.wait_ge(s["ss_sqrt"], q + 1)
                    V.reciprocal(T2, T2)
                    dve.drain()
                    V.scalar_tensor_tensor(kkn[:, :], kk_[:, :], kk_col, T2, ALU.mult, ALU.mult)
                if e == 3 and fin:
                    dve.wait_ge(s["var_sqrt"], f + 1)
                    V.reciprocal(ysq[:, :], ysq[:, :])
                    dve.drain()
                    V.tensor_tensor(yc[:, :], yc[:, :], ysq[:, :], ALU.mult)
                    dve.wait_ge(s["fprm_in"], 32 * (f + 1))
                    dve.drain()
                    V.tensor_scalar(yc[:, :], yc[:, :], col(fprm, 0), col(fprm, 1), ALU.mult, ALU.add)
                    dve.drain()
                    V.tensor_tensor(yc[:, :], yc[:, :], bonv[f % 2][:, :], ALU.add)
                    dve.wait_ge(s["gate_ev"], f + 1)
                    dve.drain()
                    V.tensor_tensor(yc[:, :], yc[:, :], gs[:, :], ALU.mult).then_inc(s["y_fin"], 1)
                if e == 3 and elem:
                    dve.wait_ge(s["g_ready"], 2 * (q + 1))
                    dve.drain()
                    V.tensor_tensor(chunks(rT[par]), chunks(rr), g_pad[:, :, 1:1 + L], ALU.mult)
                    V.scalar_tensor_tensor(chunks(aT[par]), chunks(kkn), -1.0, g_pad[:, :, 0:L],
                                           ALU.mult, ALU.mult).then_inc(s["ab_ready"], 1)
                    V.tensor_copy(g_last[:, par, :], g_pad[:, :, L:L + 1].rearrange("p c o -> p (c o)"))
                    V.tensor_tensor(aa[:, :], aa[:, :], kkn[:, :], ALU.mult)
                    V.tensor_tensor(kk_[:, :], kp[:, :], g_inv[:, :], ALU.mult).then_inc(s["kt_ready"], 1)
                    dve.drain()
                    V.tensor_tensor(aa[:, :], aa[:, :], g_inv[:, :], ALU.mult).then_inc(s["bt_ready"], 1)
                    dve.wait_ge(s["bon_mm"], q + 1)
                    V.tensor_tensor(bonv[par][:, :], bank(5), vv[:, :], ALU.mult).then_inc(s["bon_ev"], 1)
                if e == 4 and elem:
                    dve.wait_ge(s["mak_mm"], q + 1)
                    masked(makT[par], 4, mk_up[:, :]).then_inc(s["mak_ev"], 1)
                    dve.wait_ge(s["mrk_mm"], q + 1)
                    masked(mrkT[par], 5, mk_upi[:, :]).then_inc(s["mrk_ev"], 1)
                if e == 5 and elem:
                    dve.wait_ge(s["mab_mm"], q + 1)
                    masked(m_ab, 4, mk_lo[:, :]).then_inc(s["mab_ev"], 1)
                    dve.wait_ge(s["mabT_mm"], q + 1)
                    masked(m_abT, 5, mk_up[:, :]).then_inc(s["mabT_ev"], 1)
                    dve.drain()
                    V.tensor_tensor(chunks(inv), chunks(m_ab), over_chunks(mk_1[:, :]), ALU.mult)
                    V.tensor_tensor(chunks(invT[par]), chunks(m_abT), over_chunks(mk_1T[:, :]), ALU.mult)
                    dve.drain()
                    V.tensor_tensor(chunks(inv), chunks(inv), over_chunks(eye2[:, :]), ALU.add)
                    V.tensor_tensor(chunks(invT[par]), chunks(invT[par]), over_chunks(eye2[:, :]),
                                    ALU.add).then_inc(s["inv_init"], 1)
                if e >= 6 and e % 2 == 0 and elem:
                    lv = (e - 6) // 2
                    dve.wait_ge(s["t_mm"], len(LEVELS) * q + lv + 1)
                    masked(t_lev, 4, mk_lev[:, lv, :]).then_inc(s["t_ev"], 1)
                    if e == 6:
                        dve.wait_ge(s["mrb_mm"], q + 1)
                        masked(mrbT[par], 3, mk_upi[:, :]).then_inc(s["mrb_ev"], 1)
                if e >= 7 and e % 2 == 1 and elem:
                    lv = (e - 7) // 2
                    if lv < len(LEVELS) - 1:
                        dve.wait_ge(s["x_mm"], (len(LEVELS) - 1) * q + lv + 1)
                        V.tensor_tensor(inv[:, :], inv[:, :], bank(5), ALU.add).then_inc(s["x_ev"], 1)
                    dve.wait_ge(s["xT_mm"], len(LEVELS) * q + lv + 1)
                    V.tensor_tensor(invT[par][:, :], invT[par][:, :], bank(3), ALU.add).then_inc(s["xT_ev"], 1)

            for g in range(G_IN):
                c = g - 3
                chain = 0 <= c < PAIRS
                w = width_of("lora" if g == 0 else "pair")
                w_next = width_of("pair" if g + 1 < G_IN else "rest")
                for u in range(UNITS):
                    lo_next(g, u, w, w_next)
                    if g == 1 and u == 0:
                        dve.wait_ge(s["in_evac"], 3)
                        dve.wait_ge(s["lmu_in"], 16)
                        for i in range(3):
                            V.tensor_tensor(lora[:, i, :], pad[i][:, 0:SEQ], pad[i][:, 1:1 + SEQ], ALU.subtract)
                        dve.drain()
                        for i in range(3):
                            last = V.scalar_tensor_tensor(lora[:, i, :], lora[:, i, :], col(lmu, i),
                                                          pad[i][:, 1:1 + SEQ], ALU.mult, ALU.add)
                        last.then_inc(s["lora_shift"], 1)
                    if g == 1 and u == 1:
                        dve.wait_ge(s["lora_act"], 2)
                        V.tensor_scalar(lora[:, 1:3, :], lora[:, 1:3, :], 1.0, None, ALU.add)
                        dve.drain()
                        V.reciprocal(lora[:, 1:3, :], lora[:, 1:3, :]).then_inc(s["lora_act"], 1)
                    if chain and u:
                        dve.drain()
                        V.tensor_scalar(st_g[:, :], st_s[:, u % 2, :], g_last[:, c % 2, u:u + 1], None, ALU.mult)
                    gap(2 * u, g)
                    gap(2 * u + 1, g)
                    if chain and u < NC - 1:
                        dve.wait_ge(s["s_mm"], (NC - 1) * c + u + 1)
                        dst, gl = st_s[:, (u + 1) % 2, :], g_last[:, c % 2, u:u + 1]
                        if u == 0:
                            V.tensor_scalar(dst, ps[:, 6, 2 * L:3 * L], gl, None, ALU.mult).then_inc(s["s_ev"], 1)
                        else:
                            dve.drain()
                            V.scalar_tensor_tensor(dst, ps[:, 6, 2 * L:3 * L], gl, st_g[:, :],
                                                   ALU.mult, ALU.add).then_inc(s["s_ev"], 1)

            hv = h[:, :, :].rearrange("p t (q n) -> p (t q) n", n=SEQ)
            dve.wait_ge(s["y_hi"], 1)
            V.tensor_tensor(act_lo[:, 4:4 + PAIRS, :], hv[:, 8:8 + PAIRS, :], act_hi[:, 4:4 + PAIRS, :].bitcast(F32),
                            ALU.subtract).then_inc(s["y_lo"], 1)
            dve.wait_ge(s["sink_in"], 16)
            for st in range(N_UNITS_ATT + 3):
                n = st
                if n < N_UNITS_ATT:
                    kind, t, half, i, key0, keys = unit_of(n)
                    hd = n // 4
                    dve.wait_ge(s["sc_mm"], n + 1)
                    dve.wait_ge(s["bias_ready"], hd + 1)
                    if n >= 2:
                        dve.wait_ge(s["p_exp"], n - 1)
                    V.tensor_tensor_reduce(out=att_s[:, n % 2, 0:keys], in0=ps[:, n % 2, 0:keys],
                                           in1=falling(bias[:, hd % 2, 0:keys]), scale=1.0, scalar=-3e38,
                                           op0=ALU.add, op1=ALU.max,
                                           accum_out=att_c[:, n % 4, 0:1]).then_inc(s["sc_max"], 1)
                    dve.wait_ge(s["sc_max"], n + 1)
                    if kind == "C":
                        head = (t - 4) + 4 * half
                        V.tensor_scalar(att_c[:, n % 4, 1:2], att_c[:, n % 4, 0:1], sink[:, head:head + 1], -1.0,
                                        ALU.max, ALU.mult).then_inc(s["sc_neg"], 1)
                    else:
                        V.tensor_scalar(att_c[:, n % 4, 1:2], att_c[:, n % 4, 0:1], -1.0, None,
                                        ALU.mult).then_inc(s["sc_neg"], 1)
                n = st - 1
                if 0 <= n < N_UNITS_ATT:
                    kind, keys = unit_of(n)[0], unit_of(n)[5]
                    dve.wait_ge(s["p_exp"], n + 1)
                    if kind == "C":
                        V.tensor_tensor(att_c[:, n % 4, 2:3], att_c[:, n % 4, 2:3], att_c[:, n % 4, 3:4], ALU.add)
                        dve.drain()
                    V.reciprocal(att_c[:, n % 4, 0:1], att_c[:, n % 4, 2:3])
                    dve.drain()
                    V.tensor_scalar(att_p[:, n % 4, 0:keys], att_p[:, n % 4, 0:keys], att_c[:, n % 4, 0:1], None,
                                    ALU.mult).then_inc(s["p_ready"], 1)
                n = st - 3
                if n >= 0 and n % 8 == 7:
                    t = n // 8
                    mt = t if t < 4 else t + 8
                    dve.wait_ge(s["o_hi"], t + 1)
                    V.tensor_tensor(act_lo[:, mt, :], bank(4 + t % 2), act_hi[:, mt, :].bitcast(F32),
                                    ALU.subtract).then_inc(s["o_lo"], 1)

            def add_set(sidx, par, nb):
                for t in range(TT):
                    dve.wait_ge(s["bank_done"], 4 * sidx + t + 1)
                    dst = h[:, t, nb * 512:(nb + 1) * 512]
                    V.tensor_tensor(dst, dst, bank(4 * par + t), ALU.add).then_inc(s["bank_evac"], 1)

            def copy_set(sidx, dst, n, scale=1.0):
                for m in range(4):
                    dve.wait_ge(s["bank_done"], 4 * sidx + m + 1)
                    V.tensor_scalar(dst[:, m, :], ps[:, 4 * (sidx % 2) + m, 0:n], scale, None,
                                    ALU.mult).then_inc(s["bank_evac"], 1)

            R = width_of("rest")
            dve.wait_ge(s["h_in"], 16 * TT)
            for g in range(G_WOUT, G_XK):
                for u in range(UNITS):
                    lo_next(g, u, R, R)
                add_set(g - G_WOUT, (g - G_WOUT) % 2, g - G_WOUT)
            dve.wait_ge(s["mem_in"], 32)
            mem_hi = mid_hi[:, :, :].rearrange("p a (b n) -> p (a b) n", n=N_MEM)
            mem_lo = mid_lo[:, :, :].rearrange("p a (b n) -> p (a b) n", n=N_MEM)
            dve.drain()
            norm(1, memx, 2, 2, mem_hi, mem_lo, N_MEM)
            for g, sidx, dst in ((G_XK, S_XK, xk_t), (G_XV, S_XV, xv_t)):
                for u in range(UNITS):
                    lo_next(g, u, R, R)
                copy_set(sidx, dst, N_MEM)
            dve.drain()
            norm(2, h, TT, 1, act_hi, act_lo, SEQ)
            for u in range(UNITS):
                lo_next(G_XQ, u, R, R)
            copy_set(S_XQ, xq_t, SEQ, X_SCALE)
            dve.wait_ge(s["zeroed"], 2)
            for st in range(16 + 3):
                n = st
                if n < 16:
                    dve.wait_ge(s["xs_mm"], n + 1)
                    if n >= 2:
                        dve.wait_ge(s["xp_exp"], n - 1)
                    V.tensor_tensor_reduce(out=x_s[:, n % 2, :], in0=ps[:, n % 2, 0:N_MEM], in1=x_zero[:, :],
                                           scale=1.0, scalar=-3e38, op0=ALU.add, op1=ALU.max,
                                           accum_out=x_c[:, n % 4, 0:1]).then_inc(s["xs_max"], 1)
                    dve.wait_ge(s["xs_max"], n + 1)
                    V.tensor_scalar(x_c[:, n % 4, 1:2], x_c[:, n % 4, 0:1], -1.0, None, ALU.mult).then_inc(s["xs_neg"], 1)
                n = st - 1
                if 0 <= n < 16:
                    dve.wait_ge(s["xp_exp"], n + 1)
                    V.reciprocal(x_c[:, n % 4, 0:1], x_c[:, n % 4, 2:3])
                    dve.drain()
                    V.tensor_scalar(x_p[:, n % 4, :], x_p[:, n % 4, :], x_c[:, n % 4, 0:1], None,
                                    ALU.mult).then_inc(s["xp_ready"], 1)
                n = st - 3
                if n >= 0 and n % 4 == 3:
                    dve.wait_ge(s["xo_hi"], n // 4 + 1)
                    V.tensor_tensor(mid_lo[:, n // 4, :], bank(4 + (n // 4) % 2), mid_hi[:, n // 4, :].bitcast(F32),
                                    ALU.subtract).then_inc(s["xo_lo"], 1)
            for u in range(UNITS):
                lo_next(G_XO, u, R, R)
                if u % 2:
                    add_set(S_XO + u // 2, (S_XO + u // 2) % 2, u // 2)
            dve.drain()
            norm(3, h, TT, 3, act_hi, act_lo, SEQ)

            def square_tiles(c, j, tiles):
                for m in tiles:
                    r = m % 2
                    dve.wait_ge(s["relu_done"], 8 * c + 4 * j + m + 1)
                    V.scalar_tensor_tensor(sq_t[:, r, :], bank(4 * ((S_MLP + j) % 2) + m), 0.0, relu_t[:, r, :],
                                           ALU.max, ALU.mult).then_inc(s["bank_evac"], 1)
                    dve.wait_ge(s["mid_hi_done"], 8 * c + 4 * j + m + 1)
                    dve.wait_ge(s["bank_evac"], 4 * (S_MLP + 6 * c + j) + m + 1)
                    V.tensor_tensor(mid_lo[:, 4 * j + m, :], sq_t[:, r, :], mid_hi[:, 4 * j + m, :].bitcast(F32),
                                    ALU.subtract).then_inc(s["mid_done"], 1)

            def mlp_chunk(c, last):
                g0 = G_MLP + 4 * c
                for b in range(4):
                    for u in range(UNITS):
                        if b in (1, 2) and u == 0:
                            square_tiles(c, b - 1, (2, 3))
                        lo_next(g0 + b, u, R, None if last and b == 3 else R)
                        if b < 2 and u == UNITS - 1:
                            square_tiles(c, b, (0, 1))
                        if b >= 2 and u % 4 == 3:
                            nb = 2 * (b - 2) + u // 4
                            add_set(S_MLP + 6 * c + 2 + nb, (S_MLP + nb) % 2, nb)

            with dve.Fori(0, MLP_CHUNKS - 1) as c:
                mlp_chunk(c, False)
            mlp_chunk(MLP_CHUNKS - 1, True)
            dve.drain()
            norm(4, h, TT, None, None, None, SEQ)
            dve.wait_ge(s["gout_in"], 16)
            for t in range(TT):
                V.scalar_tensor_tensor(h[:, t, :], h[:, t, :], rms[:, t:t + 1], gain_out,
                                       ALU.mult, ALU.mult).then_inc(s["out_ready"], 1)

        @block.tensor
        def _(pe):
            mm = nc.tensor.matmul

            def split_mm(dst, a_hi, a_lo, b_hi, b_lo, start, stop):
                mm(dst, a_hi, b_hi, start=start, stop=False)
                mm(dst, a_hi, b_lo, start=False, stop=False)
                return mm(dst, a_lo, b_hi, start=False, stop=stop)

            def norm(k, src, tiles):
                for t in range(tiles):
                    if t == 0:
                        pe.wait_ge(s["diag_ready"], [0, TT, TT + 2, 2 * TT + 2][k] + tiles)
                for kt in range(KT):
                    if kt >= 8:
                        pe.wait_ge(s["norm_lo"], KT * k + kt - 7)
                    for t in range(tiles):
                        last = mm(ps[:, kt % 8, t * P:(t + 1) * P], src[:, t, kt * P:(kt + 1) * P], diag[:, t, :],
                                  start=True, stop=True)
                    last.then_inc(s["tr_mm"], 1)
                pe.wait_ge(s["norm_lo"], KT * (k + 1))

            def both(dst, lhsT, rhs, start, stop):
                for hf in HALF:
                    last = mm(dst[hf], lhsT[hf], rhs[hf], start=start, stop=stop)
                return last

            def grams(b, lhsT, rhs):
                for c in range(NC):
                    last = both(ps[:, b, part(c)], lhsT[:, part(c)], rhs[:, part(c)], True, True)
                return last

            def to_tokens(b, src):
                for c in range(NC):
                    last = both(ps[:, b, part(c)], src[:, part(c)], eye2, True, True)
                return last

            norm(0, x_mix, TT)
            T1 = pad[0][:, 1:1 + SEQ]
            LV = len(LEVELS)

            def gap(e, g):
                q, f = g - 2, g - 4
                elem, fin = 0 <= q < PAIRS, 0 <= f < PAIRS
                par = q % 2
                if e == 0 and elem:
                    pe.wait_ge(s["prm_in"], 16 * (q + 1))
                    pe.wait_ge(s["lora_act"], 3)
                    if q:
                        pe.wait_ge(s["t_ev"], LV * q)
                        pe.wait_ge(s["x_ev"], (LV - 1) * q)
                    mm(bank(4), prm[0:L, N_PRM:], lora[0:L, 0, :], start=True, stop=True).then_inc(s["zw_mm"], 1)
                    mm(bank(5), prm[L:P, N_PRM:], lora[L:P, 0, :], start=True, stop=True).then_inc(s["za_mm"], 1)
                if e == 0 and fin:
                    pe.wait_ge(s["y_ev"], f + 1)
                    if elem or q == PAIRS:
                        pe.wait_ge(s["xT_ev"], LV * q)
                    mm(bank(3), mean2[:, :], yb[:, :], start=True, stop=True).then_inc(s["mean_mm"], 1)
                if e == 1 and elem:
                    pe.wait_ge(s["shifted"], q + 1)
                    if fin:
                        pe.wait_ge(s["yc_ready"], f + 1)
                    elif q:
                        pe.wait_ge(s["xT_ev"], LV * q)
                    to_tokens(3, vv).then_inc(s["vtok_mm"], 1)
                    pe.wait_ge(s["sq_k"], q + 1)
                    pe.wait_ge(s["zw_ev"], q + 1)
                    mm(bank(4), ones2[:, :], T1, start=True, stop=True).then_inc(s["ss_mm"], 1)
                if e == 2 and fin:
                    pe.wait_ge(s["ysq_ready"], f + 1)
                    if elem:
                        pe.wait_ge(s["vtok_ev"], q + 1)
                        pe.wait_ge(s["za_ev"], q + 1)
                    mm(bank(3), mean2[:, :], ysq[:, :], start=True, stop=True).then_inc(s["var_mm"], 1)
                    pe.wait_ge(s["fprm_in"], 32 * (f + 1))
                    mm(bank(5), fprm[:, 2:2 + P], lora[:, 1, :], start=True, stop=False)
                    mm(bank(5), gup2[96:P, :], lora[96:P, 2, :], start=False, stop=True).then_inc(s["gate_mm"], 1)
                if e == 3 and elem:
                    pe.wait_ge(s["bon_in"], q + 1)
                    if fin:
                        pe.wait_ge(s["gate_ev"], f + 1)
                    pe.wait_ge(s["za_ev"], q + 1)
                    mm(bank(5), ones2[:, :], T1, start=True, stop=True).then_inc(s["bon_mm"], 1)
                if e == 4 and elem:
                    pe.wait_ge(s["kt_ready"], q + 1)
                    pe.wait_ge(s["vtok_ev"], q + 1)
                    if fin:
                        pe.wait_ge(s["var_eps"], f + 1)
                    to_tokens(3, kk_).then_inc(s["ktok_mm"], 1)
                    pe.wait_ge(s["ab_ready"], q + 1)
                    pe.wait_ge(s["ss_max"], q + 1)
                    grams(4, kk_, aT[par]).then_inc(s["mak_mm"], 1)
                    pe.wait_ge(s["bon_ev"], q + 1)
                    grams(5, kk_, rT[par]).then_inc(s["mrk_mm"], 1)
                if e == 5 and elem:
                    pe.wait_ge(s["bt_ready"], q + 1)
                    pe.wait_ge(s["mak_ev"], q + 1)
                    grams(4, aT[par], aa).then_inc(s["mab_mm"], 1)
                    pe.wait_ge(s["mrk_ev"], q + 1)
                    grams(5, aa, aT[par]).then_inc(s["mabT_mm"], 1)
                    pe.wait_ge(s["ktok_ev"], q + 1)
                    to_tokens(3, aa).then_inc(s["btok_mm"], 1)
                if e >= 6 and e % 2 == 0 and elem:
                    lv = (e - 6) // 2
                    pe.wait_ge(s["inv_init"], q + 1)
                    if lv:
                        pe.wait_ge(s["x_ev"], (LV - 1) * q + lv)
                    grams(4, m_abT, inv).then_inc(s["t_mm"], 1)
                    if e == 6:
                        pe.wait_ge(s["btok_ev"], q + 1)
                        grams(3, aa, rT[par]).then_inc(s["mrb_mm"], 1)
                if e >= 7 and e % 2 == 1 and elem:
                    lv = (e - 7) // 2
                    pe.wait_ge(s["t_ev"], LV * q + lv + 1)
                    if lv:
                        pe.wait_ge(s["xT_ev"], LV * q + lv)
                    if lv < LV - 1:
                        grams(5, invT[par], t_lev).then_inc(s["x_mm"], 1)
                    pe.wait_ge(s["mrb_ev"], q + 1)
                    grams(3, t_lev, invT[par]).then_inc(s["xT_mm"], 1)

            def chain_z(c, u):
                par = c % 2
                dst = ps[:, 6, 0:L]
                if u:
                    pe.wait_ge(s["s_ev"], (NC - 1) * c + u)
                last = both(dst, makT[par][:, part(u)], v_tok[par][:, part(u)], True, u == 0)
                if u:
                    last = both(dst, aT[par][:, part(u)], st_s[:, u % 2, :], False, True)
                last.then_inc(s["z_mm"], 1)

            def chain_u(c, u):
                par = c % 2
                if u == 0:
                    pe.wait_ge(s["xT_ev"], LV * (c + 1))
                pe.wait_ge(s["z_ev"], NC * c + u + 1)
                both(ps[:, 6, L:2 * L], invT[par][:, part(u)], z_s, True, True).then_inc(s["u_mm"], 1)

            def chain_sy(c, u):
                par = c % 2
                pe.wait_ge(s["u_ev"], NC * c + u + 1)
                if u < NC - 1:
                    both(ps[:, 6, 2 * L:3 * L], b_tok[par][:, part(u)], u_s, True, False)
                    both(ps[:, 6, 2 * L:3 * L], k_tok[par][:, part(u)], v_tok[par][:, part(u)], False, True).then_inc(s["s_mm"], 1)
                if u == 0 and c:
                    pe.wait_ge(s["y_ev"], c)
                dst = ps[:, 7, part(u)]
                both(dst, u_s, mrbT[par][:, part(u)], True, False)
                last = both(dst, v_tok[par][:, part(u)], mrkT[par][:, part(u)], False, u == 0)
                if u:
                    last = both(dst, st_s[:, u % 2, :], rT[par][:, part(u)], False, True)
                if u == NC - 1:
                    last.then_inc(s["y_mm"], 1)

            for g in range(G_IN):
                c = g - 3
                chain = 0 <= c < PAIRS
                w = LORA_W if g == 0 else PAIR_W
                cols = (0, P, 160) if g == 0 else (0, P, 2 * P)
                for u in range(UNITS):
                    pe.wait_ge(s["w_split"], UNITS * g + u + 1)
                    wh = w_hi[:, u % SPL, 0:2 * w].rearrange("p (c n) -> p c n", c=2)
                    wl = w_lo[:, u % SPL, 0:2 * w].rearrange("p (c n) -> p c n", c=2)
                    combos = [(k, m) for k in range(2) for m in range(3)]
                    for third in range(3):
                        if chain and third == 0:
                            chain_z(c, u)
                        if chain and third == 1:
                            chain_u(c, u)
                        if third < 2:
                            gap(2 * u + third, g)
                        else:
                            if chain:
                                chain_sy(c, u)
                        for k, m in combos[2 * third:2 * third + 2]:
                            kt = 2 * u + k
                            if kt == 0 and g:
                                pe.wait_ge(s["in_evac"], 3 * (g - 1) + m + 1)
                            cs_ = slice(cols[m], cols[m] + P)
                            last = split_mm(bank(m), wh[:, k, cs_], wl[:, k, cs_], act_hi[:, kt, :], act_lo[:, kt, :],
                                            kt == 0, kt == KT - 1)
                            if kt == KT - 1:
                                last.then_inc(s["in_done"], 1)
                            elif third == 2 and (k, m) == combos[-1]:
                                last.then_inc(s["w_used"], 1)
                    if u == UNITS - 1:
                        pe.drain().then_inc(s["w_used"], 1)

            hv = h[:, :, :].rearrange("p t (q n) -> p (t q) n", n=SEQ)
            pe.wait_ge(s["vy_in"], 16 * 13)
            pe.wait_ge(s["in_evac"], 3 * G_IN)
            flat67 = ps[:, 6:8, :].rearrange("p a b -> p (a b)")
            for kb in range(TT):
                if kb:
                    pe.wait_ge(s["vt_ev"], kb)
                for ft in range(5):
                    last = nc.tensor.transpose(flat67[:, ft * P:(ft + 1) * P], hv[:, ft, kb * P:(kb + 1) * P], ident[:, :])
                last.then_inc(s["vt_mm"], 1)
            pe.wait_ge(s["vt_ev"], TT)
            for st in range(N_UNITS_ATT + 3):
                n = st
                if n < N_UNITS_ATT:
                    kind, t, half, i, key0, keys = unit_of(n)
                    if n % 8 == 0:
                        pe.wait_ge(s["qk_in"], 32 * (t + 1))
                    if n >= 2:
                        pe.wait_ge(s["sc_max"], n - 1)
                    hf = HALF[half]
                    mm(ps[:, n % 2, 0:keys], qk[hf, t % 2, 0, i * P:(i + 1) * P], qk[hf, t % 2, 1, key0:key0 + keys],
                       start=True, stop=True).then_inc(s["sc_mm"], 1)
                n = st - 2
                if 0 <= n < N_UNITS_ATT:
                    keys = unit_of(n)[5]
                    pe.wait_ge(s["p_ready"], n + 1)
                    if n >= 2:
                        pe.wait_ge(s["pT_ev"], n - 1)
                    for b in range(keys // P):
                        last = nc.tensor.transpose(ps[:, 2 + n % 2, b * P:(b + 1) * P],
                                                   att_p[:, n % 4, b * P:(b + 1) * P], ident[:, :])
                    last.then_inc(s["pT_mm"], 1)
                n = st - 3
                if n >= 0:
                    kind, t, half, i, key0, keys = unit_of(n)
                    pe.wait_ge(s["pT_ev"], n + 1)
                    if n % 8 == 0 and t >= 2:
                        pe.wait_ge(s["o_lo"], t - 1)
                    v0 = t * P + half * L if kind == "A" else 512 + half * L
                    nb = keys // P
                    for b in range(nb):
                        last = mm(ps[HALF[half], 4 + t % 2, i * P:(i + 1) * P], vt[:, key0 // P + b, v0:v0 + L],
                                  att_pT[:, n % 2, b * P:(b + 1) * P], start=b == 0, stop=b == nb - 1)
                    last.then_inc(s["o_mm"], 1)

            def rest_unit(n, u, stationary, a_hi, a_lo, kts, cols, sidx, par, first, last_kt, free):
                pe.wait_ge(s["w_split"], n + 1)
                wh = w_hi[:, u % SPL, :].rearrange("p (c n) -> p c n", c=2)
                wl = w_lo[:, u % SPL, :].rearrange("p (c n) -> p c n", c=2)
                for k, kt in enumerate(kts):
                    for m in range(4):
                        mp = slice(m * P, (m + 1) * P)
                        if kt == first and free:
                            pe.wait_ge(s["bank_evac"], 4 * (sidx - 2) + m + 1)
                        start, stop = kt == first, kt == last_kt
                        if stationary == "w":
                            last = split_mm(ps[:, 4 * par + m, 0:cols], wh[:, k, mp], wl[:, k, mp],
                                            a_hi[:, kt, :], a_lo[:, kt, :], start, stop)
                        else:
                            last = split_mm(bank(4 * par + m), a_hi[:, kt, mp], a_lo[:, kt, mp], wh[:, k, :], wl[:, k, :],
                                            start, stop)
                        if stop:
                            last.then_inc(s["bank_done"], 1)
                if last_kt in kts:
                    pe.drain().then_inc(s["w_used"], 1)
                else:
                    last.then_inc(s["w_used"], 1)

            pe.wait_ge(s["o_lo"], 8)
            pe.wait_ge(s["y_lo"], 1)
            for g in range(G_WOUT, G_XK):
                sidx = g - G_WOUT
                for u in range(UNITS):
                    rest_unit(UNITS * g + u, u, "a", act_hi, act_lo, (2 * u, 2 * u + 1), 512, sidx, sidx % 2, 0, KT - 1,
                              sidx >= 2)
            mem_hi = mid_hi[:, :, :].rearrange("p a (b n) -> p (a b) n", n=N_MEM)
            mem_lo = mid_lo[:, :, :].rearrange("p a (b n) -> p (a b) n", n=N_MEM)
            norm(1, memx, 2)
            for g, sidx in ((G_XK, S_XK), (G_XV, S_XV)):
                for u in range(UNITS):
                    rest_unit(UNITS * g + u, u, "w", mem_hi, mem_lo, (2 * u, 2 * u + 1), N_MEM, sidx, sidx % 2, 0, KT - 1,
                              True)
            norm(2, h, TT)
            for u in range(UNITS):
                rest_unit(UNITS * G_XQ + u, u, "w", act_hi, act_lo, (2 * u, 2 * u + 1), SEQ, S_XQ, S_XQ % 2, 0, KT - 1, True)
            for kb in range(2):
                if kb:
                    pe.wait_ge(s["xvt_ev"], kb)
                for t in range(4):
                    last = nc.tensor.transpose(ps[:, 6, t * P:(t + 1) * P], xv_t[:, t, kb * P:(kb + 1) * P], ident[:, :])
                last.then_inc(s["xvt_mm"], 1)
            pe.wait_ge(s["xvt_ev"], 2)
            pe.wait_ge(s["bank_evac"], 4 * S_XO)
            for st in range(16 + 3):
                n = st
                if n < 16:
                    if n >= 2:
                        pe.wait_ge(s["xs_max"], n - 1)
                    mm(ps[:, n % 2, 0:N_MEM], xq_t[:, n // 4, (n % 4) * P:(n % 4 + 1) * P], xk_t[:, n // 4, :],
                       start=True, stop=True).then_inc(s["xs_mm"], 1)
                n = st - 2
                if 0 <= n < 16:
                    pe.wait_ge(s["xp_ready"], n + 1)
                    if n >= 2:
                        pe.wait_ge(s["xpT_ev"], n - 1)
                    for b in range(2):
                        last = nc.tensor.transpose(ps[:, 2 + n % 2, b * P:(b + 1) * P], x_p[:, n % 4, b * P:(b + 1) * P],
                                                   ident[:, :])
                    last.then_inc(s["xpT_mm"], 1)
                n = st - 3
                if n >= 0:
                    t, i = n // 4, n % 4
                    pe.wait_ge(s["xpT_ev"], n + 1)
                    if i == 0 and t >= 2:
                        pe.wait_ge(s["xo_lo"], t - 1)
                    for b in range(2):
                        last = mm(ps[:, 4 + t % 2, i * P:(i + 1) * P], xv_tok[:, b, t * P:(t + 1) * P],
                                  x_pT[:, n % 2, b * P:(b + 1) * P], start=b == 0, stop=b == 1)
                    last.then_inc(s["xo_mm"], 1)
            pe.wait_ge(s["xo_lo"], 4)
            for u in range(UNITS):
                nb, k0 = u // 2, 2 * (u % 2)
                rest_unit(UNITS * G_XO + u, u, "a", mid_hi, mid_lo, (k0, k0 + 1), 512, S_XO + nb, (S_XO + nb) % 2, 0, 3, True)
            norm(3, h, TT)

            def mlp_chunk(c):
                g0 = G_MLP + 4 * c
                for b in range(2):
                    for u in range(UNITS):
                        rest_unit(UNITS * (g0 + b) + u, u, "w", act_hi, act_lo, (2 * u, 2 * u + 1), SEQ,
                                  S_MLP + 6 * c + b, (S_MLP + b) % 2, 0, KT - 1, True)
                for v in range(2 * UNITS):
                    nb, k0 = v // 4, 2 * (v % 4)
                    if nb == 0:
                        pe.wait_ge(s["mid_done"], FT * c + k0 + 2)
                    rest_unit(UNITS * (g0 + 2) + v, v % UNITS, "a", mid_hi, mid_lo, (k0, k0 + 1), 512,
                              S_MLP + 6 * c + 2 + nb, (S_MLP + nb) % 2, 0, FT - 1, True)

            with pe.Fori(0, MLP_CHUNKS) as c:
                mlp_chunk(c)


def kernel(x, mem, norm_mix, w_in, w_vres_down, w_out, a_rel_bias, rwkv_mu, rwkv_mu_vres, rwkv_w0, rwkv_w_up, rwkv_a0,
           rwkv_a_up, rwkv_v0, rwkv_v_up, rwkv_g_up, rwkv_k_k, rwkv_k_a, rwkv_r_k, rwkv_ln_w, rwkv_ln_b, c_sinks,
           t5_bias, norm_x, norm_mem, x_wq, x_wk, x_wv, x_wo, norm_mlp, mlp_w1, mlp_w2, norm_final):
    import math

    import concourse.bacc as _bacc
    from concourse.bass_utils import run_bass_kernel_spmd as _run

    def units(w):
        rows, cols = w.shape
        return w.reshape(rows // (2 * P), 2, P, cols).transpose(0, 2, 1, 3).reshape(rows // (2 * P), P, 2 * cols)

    def by_columns(w, n):
        return [units(w[:, j:j + n]) for j in range(0, w.shape[1], n)]

    arr = np.asarray
    wi, wo = arr(w_in)[0], arr(w_out)[0]
    b_off, b_w = 1536, 1024
    c_off = b_off + 3 * b_w + LORA_W
    pair_of = [np.concatenate([wi[:, b_off + j * b_w + p * P:b_off + j * b_w + (p + 1) * P] for j in range(3)], axis=1)
               for p in range(PAIRS)]
    q_cols = np.concatenate([np.arange(hd * L, (hd + 1) * L) for t in range(4) for hd in (t, 4 + t)])
    w_c = np.concatenate([wi[:, c_off + q_cols], wi[:, c_off + 512:c_off + 768]], axis=1)
    w_lora = units(wi[:, b_off + 3 * b_w:c_off])
    w_pairs = np.concatenate([units(w) for w in pair_of] + by_columns(wi[:, 0:b_off], PAIR_W) + by_columns(w_c, PAIR_W))
    wo_p = np.concatenate([wo[0:1536], wo[1536 + q_cols]])
    w1, w2 = arr(mlp_w1)[0], arr(mlp_w2)[0]
    mlp = []
    for c in range(MLP_CHUNKS):
        f = slice(c * FT * P, (c + 1) * FT * P)
        mlp += by_columns(w1[:, f], REST_W) + by_columns(w2[f], REST_W)
    w_rest = np.concatenate(by_columns(wo_p, REST_W) + [units(arr(x_wk)[0]), units(arr(x_wv)[0]), units(arr(x_wq)[0])]
                            + by_columns(arr(x_wo)[0], REST_W) + mlp)

    def feature(v):
        return arr(v).reshape(-1, P).T

    mu = arr(rwkv_mu)[0]
    vecs = [mu[0:1024], mu[1024:2048], mu[2048:3072], arr(rwkv_w0)[0], arr(rwkv_a0)[0], arr(rwkv_k_k)[0],
            arr(rwkv_k_a)[0], arr(rwkv_r_k)[0].reshape(-1)]
    prm = np.stack([v.reshape(PAIRS, P) for v in vecs], axis=2)
    wa_up = np.concatenate([arr(rwkv_w_up)[0], arr(rwkv_a_up)[0]], axis=0).reshape(P, PAIRS, P).transpose(1, 0, 2)
    g_up = arr(rwkv_g_up)[0].reshape(160, PAIRS, P).transpose(1, 0, 2)
    fin = np.stack([arr(rwkv_ln_w)[0].reshape(PAIRS, P), arr(rwkv_ln_b)[0].reshape(PAIRS, P)], axis=2)
    mul = mu[3072:]
    rel_a = np.clip(np.arange(A_KEYS + P - 1) - (P - 1), -128, 128) + 128
    dist = (P - 1) - np.arange(C_KEYS + P - 1)
    near = np.abs(dist)
    large = 8 + (np.log(np.maximum(near, 1) / 8) / math.log(128 / 8) * 8).astype(np.int32)
    bucket = (dist > 0) * 16 + np.where(near < 8, near, np.minimum(large, 15))
    data = {
        "x": arr(x)[0], "mem": arr(mem)[0],
        "gains": np.stack([feature(arr(v)[0]) for v in (norm_mix, norm_x, norm_mem, norm_mlp)], axis=1),
        "w_lora": w_lora, "w_pairs": w_pairs, "w_rest": w_rest,
        "pair_prm": np.concatenate([prm, wa_up], axis=2),
        "fin_prm": np.concatenate([fin, g_up[:, 0:P]], axis=2), "gup_tail": g_up[:, P:],
        "lora_mu": np.stack([mul[0:P], mul[P:2 * P], mul[160:288]], axis=1),
        "a_line": arr(a_rel_bias)[0][rel_a].T, "c_line": arr(t5_bias)[bucket].T,
        "sinks": arr(c_sinks), "norm_final": arr(norm_final).reshape(1, D),
    }
    data = {f"in_{k}": np.ascontiguousarray(v) for k, v in data.items()}
    nc = _bacc.Bacc("TRN2", target_bir_lowering=False, num_devices=1)
    args = [nc.dram_tensor(k, v.shape, mybir.dt.from_np(v.dtype), kind="ExternalInput").ap() for k, v in data.items()]
    out = nc.dram_tensor("out_0", (SEQ, D), F32, kind="ExternalOutput").ap()
    hybrid_layer(nc, *args, out)
    r = _run(nc, [data], core_ids=[0])
    return r.results[0]["out_0"].reshape(1, SEQ, D)
```

```python
from contextlib import ExitStack

import numpy as np

import concourse.bass as bass
from concourse import mybir

F32 = mybir.dt.float32
F32R = mybir.dt.float32r
ALU = mybir.AluOpType
ACT = mybir.ActivationFunctionType

P = 128
SEQ, D, N_MEM, D_FF = 512, 2048, 256, 8192
TT = SEQ // P
KT = D // P
L = 64
NC = SEQ // L
PAIRS = 8
A_TILES = 12
C_TILES = 6
QKV = A_TILES + C_TILES
UNITS = 8
RAW = 4
LORA_W, PAIR_W, REST_W = 288, 384, 512
SPL_IN, SPL = 3, 2
SPLIT_W = max(SPL_IN * 2 * PAIR_W, SPL * 2 * REST_W)
G_C = 1
G_PAIR = G_C + C_TILES // 3
G_A = G_PAIR + PAIRS
G_IN = G_A + A_TILES // 3
G_XK, G_XV = G_IN, G_IN + 1
G_WR, G_WA = G_IN + 2, G_IN + 4
G_XQ, G_XO, G_MLP = G_IN + 6, G_IN + 7, G_IN + 8
MLP_CHUNKS = 8
G_ALL = G_MLP + 4 * MLP_CHUNKS
FT = D_FF // MLP_CHUNKS // P
RMS_EPS, GN_EPS = 1e-5, 64e-5
LOGW = float(np.exp(-0.5))
MASKED = -1e30
A_KEYS, C_KEYS = 512, 256
N_UNITS_ATT = 64
X_SCALE = 128.0 ** -0.5
MU_R, MU_K, MU_V, W0, A0, K_K, K_A, R_K, N_PRM = range(9)
HALF_W0, HALF_A0, ONE_MINUS_KA = range(3)
LEVELS = [2, 4, 8, 16, 32]


def hybrid_layer(nc, x, mem, gains, w_lora, w_pairs, w_rest, pair_prm, fin_prm, gup_tail, lora_mu,
                 a_line, c_line, sinks, norm_final, out):
    top = ExitStack()
    with top:
        def alloc(stack):
            return lambda name, shape, dt=F32: stack.enter_context(nc.sbuf_tensor(name, shape, dt))

        def sem(name):
            return top.enter_context(nc.semaphore(name))

        sb = alloc(top)
        act_hi = sb("act_hi", [P, KT, SEQ], F32R)
        act_lo = sb("act_lo", [P, KT, SEQ], F32R)
        w_raw = sb("w_raw", [P, RAW, 2 * REST_W])
        w_hi = sb("w_hi", [P, SPLIT_W], F32R)
        w_lo = sb("w_lo", [P, SPLIT_W], F32R)
        ident = sb("ident", [P, P])
        gain = sb("gain", [P, 4, KT])
        diag = sb("diag", [P, TT, P])
        ssq = sb("ssq", [P, TT, 4])
        tiny = sb("tiny", [P, 1])
        rms = sb("rms", [P, 8])
        ps = top.enter_context(nc.psum_tensor("ps", [P, 8, 512], F32))
        scr_y = nc.dram_tensor("scr_y", (PAIRS, P, SEQ), F32).ap()
        scr_qkv = nc.dram_tensor("scr_qkv", (QKV // 3, 3, P, SEQ), F32).ap()

        lay1, lay2, lay3 = ExitStack(), ExitStack(), ExitStack()
        s1 = alloc(lay1)
        x_mix = s1("x_mix", [P, TT, D])
        x_sq = s1("x_sq", [P, D])
        lay1.close()

        s2 = alloc(lay2)
        rr, kk_, vv = s2("r_s", [P, SEQ]), s2("k_s", [P, SEQ]), s2("v_s", [P, SEQ])
        sg, aa, cs = s2("sig_w", [P, SEQ]), s2("a_gate", [P, SEQ]), s2("cum_sig", [P, SEQ])
        g_pad = s2("g_pad", [P, NC, L + 1])
        g_inv = s2("g_inv", [P, SEQ])
        kkn, kp, kk_dec = s2("kk_norm", [P, SEQ]), s2("k_mod", [P, SEQ]), s2("k_dec", [P, SEQ])
        m_ab, m_abT = s2("m_ab", [P, SEQ]), s2("m_abT", [P, SEQ])
        inv, t_lev = s2("inv", [P, SEQ]), s2("t_level", [P, SEQ])
        yb, yc, ysq, gs = s2("y_raw", [P, SEQ]), s2("y_cent", [P, SEQ]), s2("y_sq", [P, SEQ]), s2("gate", [P, SEQ])
        two = lambda name: [s2(f"{name}{i}", [P, SEQ]) for i in range(2)]
        rT, aT, b_tok, k_tok, v_tok = two("r_dec"), two("a_dec"), two("b_tok"), two("k_tok"), two("v_tok")
        makT, mrbT, mrkT, invT = two("makT"), two("mrbT"), two("mrkT"), two("invT")
        bonv = [s2(f"bonus_v{i}", [P, SEQ]) for i in range(3)]
        g_last = s2("g_last", [P, 2, NC])
        z_s, u_s = s2("z_s", [P, L]), s2("u_s", [P, L])
        st_s, st_g = s2("state", [P, 2, L]), s2("state_decayed", [P, L])
        prm, prm2 = s2("prm", [P, N_PRM + P]), s2("prm2", [P, 3])
        fprm, gup2 = s2("fprm", [P, 2 + P]), s2("gup2", [P, P])
        lora = s2("lora", [P, 3, SEQ])
        lmu = s2("lora_mu", [P, 3])
        rm = s2("restart", [P, SEQ])
        eye2, ones2, mean2 = s2("eye2", [P, L]), s2("ones2", [P, P]), s2("mean2", [P, P])
        mk_up, mk_upi, mk_lo, mk_1, mk_1T = (s2(n, [P, L]) for n in ("mk_up", "mk_upi", "mk_lo", "mk_1", "mk_1T"))
        mk_lev = s2("mk_lev", [P, len(LEVELS), L])
        pad = [s2(f"pad{i}", [P, 1 + SEQ]) for i in range(3)]
        m128 = s2("m128", [P, 10, P])
        lay2.close()

        s3 = alloc(lay3)
        h = s3("h", [P, TT, D])
        mid_hi = s3("mid_hi", [P, FT, SEQ], F32R)
        mid_lo = s3("mid_lo", [P, FT, SEQ], F32R)
        memx = h[:, 0:2, :]
        y_in = h[:, 2:4, :].rearrange("p t (q n) -> p (t q) n", n=SEQ)
        xk_t, xv_t = s3("xk_t", [P, 4, N_MEM]), s3("xv_t", [P, 4, N_MEM])
        x_tmp = ExitStack()
        s4 = alloc(x_tmp)
        qk = s4("qk", [P, 2, 2, SEQ])
        bias = s4("bias", [P, 2, A_KEYS])
        vt = s4("vt", [P, TT, 640])
        att_p = s4("att_p", [P, 4, A_KEYS])
        att_pT = s4("att_pT", [P, 2, A_KEYS])
        att_c = s4("att_c", [P, 4, 4])
        sink = s4("sink", [P, 8])
        x_tmp.close()
        s6 = alloc(lay3)
        xq_t = s6("xq_t", [P, 4, SEQ])
        xv_tok = s6("xv_tok", [P, 2, 512])
        x_zero = s6("x_zero", [P, N_MEM])
        x_s, x_p, x_pT = s6("x_s", [P, 2, N_MEM]), s6("x_p", [P, 4, N_MEM]), s6("x_pT", [P, 2, N_MEM])
        x_c = s6("x_c", [P, 4, 4])
        relu_t, sq_t = s6("relu_t", [P, 2, SEQ]), s6("sq_t", [P, 2, SEQ])
        gain_out = w_raw[:, 0:2, :].rearrange("p a b -> p (a b)")
        lay3.close()

        s = {n: sem(n) for n in """
            gain_in line_in prm_in fprm_in lmu_in consts zeroed pool_step
            ssq_act ssq_dve ms_ready rms_sqrt diag_ready tr_mm norm_hi norm_lo
            w_hi_done w_split w_used in_evac lora_shift lora_act
            small_prm shifted zw_mm za_mm zw_ev za_ev sq_k ss_mm ss_max ss_sqrt cum_ready g_ready e_ready bon_in bon_mm bon_ev
            vtok_mm vtok_ev ktok_mm ktok_ev btok_mm btok_ev ab_ready kt_ready bt_ready
            mak_mm mak_ev mrk_mm mrk_ev mrb_mm mrb_ev mab_mm mabT_mm mab_ev mabT_ev inv_init
            t_mm t_ev x_mm x_ev xT_mm xT_ev
            z_mm z_ev u_mm u_ev s_mm s_ev y_mm y_ev mean_mm yc_ready ysq_ready var_mm var_eps var_sqrt rstd_ready gate_mm gate_ev y_fin y_stored
            qkv_stored v_in y_landed y_hi y_lo vt_mm vt_ev qk_in bias_in bias_ready sink_in
            sc_mm sc_max sc_neg p_exp p_ready pT_mm pT_ev o_mm o_hi o_lo
            h_in mem_in gout_in bank_evac xs_mm xs_max xs_neg xp_exp xp_ready xpT_mm xpT_ev xo_mm xo_hi xo_lo xvt_mm xvt_ev
            relu_done mid_hi_done mid_done out_ready out_stored
            """.split()}
        x_in = [sem(f"x_in{t}") for t in range(TT)]
        w_landed = [sem(f"w_landed{i}") for i in range(RAW)]

        def part(c):
            return slice(c * L, (c + 1) * L)

        HALF = (slice(0, L), slice(L, P))

        def chunks(buf):
            return buf[:, :].rearrange("p (c t) -> p c t", c=NC)

        def bank(b):
            return ps[:, b, :]

        def falling(v):
            return v[:, ::-1]

        def over_chunks(m):
            return m.rearrange("p (o t) -> p o t", o=1).to_broadcast([P, NC, L])

        def col(buf, i):
            return buf[:, i:i + 1]

        def width_of(kind):
            return 2 * {"lora": LORA_W, "pair": PAIR_W, "rest": REST_W}[kind]

        def in_slot(buf, n):
            first = n % SPL_IN * 2 * PAIR_W
            return buf[:, first:first + width_of("lora" if n < UNITS else "pair")]

        def rest_slot(buf, u):
            return buf[:, u % SPL * 2 * REST_W:(u % SPL + 1) * 2 * REST_W]

        def stages(g):
            q = g - G_PAIR - 1
            return [(i, 0 <= i < PAIRS) for i in (q, q - 1, q - 2)]

        def qkv_block(g):
            if G_C <= g < G_PAIR:
                return A_TILES // 3 + g - G_C, g - G_C
            if G_A <= g < G_IN:
                return g - G_A, C_TILES // 3 + g - G_A
            return None, None

        S_XK, S_XV, S_WR, S_WA, S_XQ, S_XO, S_MLP = 0, 1, 2, 6, 10, 11, 15
        RWKV_KT = list(range(4, 12))
        ATT_KT = [0, 1, 2, 3, 12, 13, 14, 15]

        def att_steps(v):
            if v < 4:
                return []
            steps_ = [2 * (v - 4) + i for i in range(2)] if v < 16 else [24 + 3 * (v - 16) + i for i in range(3)]
            return [st for st in steps_ if st < N_UNITS_ATT + 3]

        def mem_tiles(p, g):
            return range(2 * (p - 13), 2 * (p - 12)) if g == G_IN - 1 and 13 <= p < 21 else ()

        def mem_bank(kt):
            return 3 + kt % 5

        def a_window(i):
            return 0, P * (i + 1)

        def c_window(i):
            return (0, P) if i == 0 else (P * (i - 1), 2 * P)

        def unit_of(n):
            t, half, i = n // 8, (n // 4) % 2, n % 4
            return (("A", t, half, i) + a_window(i)) if n < 32 else (("C", t, half, i) + c_window(i))

        block = top.enter_context(nc.Block())

        @block.sync
        def _(sp):
            def unit(n_wait, slot, dst_w, src):
                if n_wait is not None:
                    sp.wait_ge(s["w_split"], n_wait)
                sp.dma_start(w_raw[:, slot, 0:dst_w], src).then_inc(w_landed[slot], 16)

            for t in range(TT):
                sp.dma_start(x_mix[:, t, :], x[t * P:(t + 1) * P, :]).then_inc(x_in[t], 16)
            for u in range(UNITS):
                unit(u - RAW + 1 if u >= RAW else None, u % RAW, width_of("lora"), w_lora[u])
            with sp.Fori(0, G_IN - 1) as j:
                for u in range(UNITS):
                    unit(UNITS * (j + 1) + u - RAW + 1, u % RAW, width_of("pair"),
                         w_pairs[bass.ds(UNITS * j + u, 1)].rearrange("o p n -> p (o n)"))
            with sp.Fori(0, G_ALL - G_IN) as j:
                for u in range(UNITS):
                    unit(UNITS * (j + G_IN) + u - RAW + 1, u % RAW, width_of("rest"),
                         w_rest[bass.ds(UNITS * j + u, 1)].rearrange("o p n -> p (o n)"))
            for t in range(TT):
                sp.wait_ge(s["out_ready"], t + 1)
                sp.dma_start(out[t * P:(t + 1) * P, :], h[:, t, :]).then_inc(s["out_stored"], 16)
            sp.wait_ge(s["out_stored"], 16 * TT)

        @block.gpsimd
        def _(pool):
            steps = [0]

            def step(ins):
                steps[0] += 1
                ins.then_inc(s["pool_step"], 1)
                pool.wait_ge(s["pool_step"], steps[0])

            pool.dma_start(gain[:, :, :], gains).then_inc(s["gain_in"], 16)
            step(nc.gpsimd.memset(ident[:, :], 0.0))
            step(nc.gpsimd.affine_select(out=ident[:, :], in_=ident[:, :], compare_op=ALU.not_equal, fill=1.0,
                                         base=0, pattern=[[-1, P]], channel_multiplier=1))
            pool.sem_inc(s["zeroed"], 1)
            pool.wait_ge(s["tr_mm"], KT)
            pool.dma_start(prm[:, :], pair_prm[0]).then_inc(s["prm_in"], 16)
            pool.dma_start(fprm[:, :], fin_prm[0]).then_inc(s["fprm_in"], 16)
            pool.dma_start(gup2[96:P, :], gup_tail[0]).then_inc(s["fprm_in"], 16)
            pool.dma_start(lmu[:, :], lora_mu).then_inc(s["lmu_in"], 16)
            for i, (cmp, base) in enumerate(((ALU.is_gt, 0), (ALU.is_ge, 0))):
                step(nc.gpsimd.memset(m128[:, i, :], 1.0))
                step(nc.gpsimd.affine_select(out=m128[:, i, :], in_=m128[:, i, :], compare_op=cmp, fill=0.0,
                                             base=base, pattern=[[1, P]], channel_multiplier=-1))
            step(nc.gpsimd.memset(m128[:, 2, :], 1.0))
            step(nc.gpsimd.affine_select(out=m128[:, 2, :], in_=m128[:, 2, :], compare_op=ALU.is_gt, fill=0.0,
                                         base=0, pattern=[[-1, P]], channel_multiplier=1))
            def level(dst, b, transposed):
                step(nc.gpsimd.memset(dst, 0.0))
                v = dst.rearrange("p (n t) -> p n t", t=2 * b)
                step(nc.gpsimd.memset(v[:, :, b:2 * b] if transposed else v[:, :, 0:b], 1.0))
                lo, hi = (0, b - 1) if transposed else (b, 2 * b - 1)
                step(nc.gpsimd.affine_select(out=v, in_=v, compare_op=ALU.is_ge, fill=0.0, base=-lo,
                                             pattern=[[-2 * b, P // (2 * b)], [0, 2 * b]], channel_multiplier=1))
                step(nc.gpsimd.affine_select(out=v, in_=v, compare_op=ALU.is_ge, fill=0.0, base=hi,
                                             pattern=[[2 * b, P // (2 * b)], [0, 2 * b]], channel_multiplier=-1))
            level(m128[:, 3, :], 1, False)
            level(m128[:, 4, :], 1, True)
            for i, b in enumerate(LEVELS):
                level(m128[:, 5 + i, :], b, False)
            for dst, src in ((mk_up, 0), (mk_upi, 1), (mk_lo, 2), (mk_1, 3), (mk_1T, 4)):
                for hf in HALF:
                    step(nc.gpsimd.tensor_copy(dst[hf, :], m128[hf, src, hf]))
            for i in range(len(LEVELS)):
                for hf in HALF:
                    step(nc.gpsimd.tensor_copy(mk_lev[hf, i, :], m128[hf, 5 + i, hf]))
            for hf in HALF:
                step(nc.gpsimd.tensor_copy(eye2[hf, :], ident[hf, hf]))
            step(nc.gpsimd.memset(ones2[:, :], 0.0))
            step(nc.gpsimd.memset(mean2[:, :], 0.0))
            for hf in HALF:
                step(nc.gpsimd.memset(ones2[hf, hf], 1.0))
                step(nc.gpsimd.memset(mean2[hf, hf], 1.0 / L))
            step(nc.gpsimd.memset(rm[:, :], 1.0))
            step(nc.gpsimd.memset(chunks(rm)[:, :, 0:1], 0.0))
            for i in range(3):
                step(nc.gpsimd.memset(pad[i][:, 0:1], 0.0))
            step(nc.gpsimd.memset(g_pad[:, :, 0:1], 1.0))
            pool.sem_inc(s["consts"], 1)
            for g in range(G_C, G_IN):
                (q, elem), _, (f, fin) = stages(g)
                if elem and q < PAIRS - 1:
                    pool.wait_ge(s["bon_ev"], q + 1)
                    pool.dma_start(prm[:, :], pair_prm[q + 1]).then_inc(s["prm_in"], 16)
                if fin:
                    pool.wait_ge(s["rstd_ready"], f + 1)
                    step(nc.gpsimd.tensor_tensor(yc[:, :], yc[:, :], ysq[:, :], ALU.mult))
                    pool.wait_ge(s["fprm_in"], 32 * (f + 1))
                    step(nc.gpsimd.tensor_scalar(yc[:, :], yc[:, :], col(fprm, 0), col(fprm, 1), ALU.mult, ALU.add))
                    step(nc.gpsimd.tensor_tensor(yc[:, :], yc[:, :], bonv[f % 3][:, :], ALU.add))
                    pool.wait_ge(s["gate_ev"], f + 1)
                    nc.gpsimd.tensor_tensor(yc[:, :], yc[:, :], gs[:, :], ALU.mult).then_inc(s["y_fin"], 1)
                    pool.wait_ge(s["y_fin"], f + 1)
                    pool.dma_start(scr_y[f], yc[:, :]).then_inc(s["y_stored"], 16)
                    if f < PAIRS - 1:
                        pool.dma_start(fprm[:, :], fin_prm[f + 1]).then_inc(s["fprm_in"], 16)
                        pool.dma_start(gup2[96:P, :], gup_tail[f + 1]).then_inc(s["fprm_in"], 16)
                if g == G_IN - 1:
                    pool.wait_ge(s["y_stored"], 16 * PAIRS)
                    for t in range(2):
                        pool.dma_start(memx[:, t, :], mem[t * P:(t + 1) * P, :]).then_inc(s["mem_in"], 16)
                    pool.wait_ge(s["qkv_stored"], 48 * (QKV // 3 - 1))
                    for i, t in enumerate((8, A_TILES + 5)):
                        pool.dma_start(att_pT[:, i, :], scr_qkv[t // 3, t % 3]).then_inc(s["v_in"], 16)
                b, _ = qkv_block(g)
                if b is not None and g < G_IN - 1:
                    pool.wait_ge(s["in_evac"], 3 * (g + 1))
                    for m in range(3):
                        pool.dma_start(scr_qkv[b, m], pad[m][:, 1:1 + SEQ]).then_inc(s["qkv_stored"], 16)
            pool.dma_start(sink[:, :], sinks.to_broadcast([P, 8])).then_inc(s["sink_in"], 16)
            for t in range(8):
                qt, kt = (t, 4 + t) if t < 4 else (A_TILES + t - 4, A_TILES + 4)
                if t >= 2:
                    pool.wait_ge(s["sc_mm"], 8 * (t - 1))
                pool.dma_start(qk[:, t % 2, 0, :], scr_qkv[qt // 3, qt % 3]).then_inc(s["qk_in"], 16)
                pool.dma_start(qk[:, t % 2, 1, :], scr_qkv[kt // 3, kt % 3]).then_inc(s["qk_in"], 16)
                for half in range(2):
                    n = 2 * t + half
                    line, w = (a_line, A_KEYS) if t < 4 else (c_line, C_KEYS)
                    head = n if t < 4 else (t - 4) + 4 * half
                    if n == 1:
                        for f in range(PAIRS):
                            pool.dma_start(y_in[:, f, :], scr_y[f]).then_inc(s["y_landed"], 16)
                    if n == 5:
                        pool.wait_ge(s["y_lo"], PAIRS)
                        pool.wait_ge(s["tr_mm"], 2 * KT)
                        for i in range(TT):
                            pool.dma_start(h[:, i, :], x[i * P:(i + 1) * P, :]).then_inc(s["h_in"], 16)
                    if n >= 2:
                        pool.wait_ge(s["sc_max"], 4 * (n - 1))
                    hankel = bass.AP(line.tensor, line[head, 0:1].offset, [[1, P], [1, w]])
                    pool.dma_start(bias[:, n % 2, 0:w], hankel).then_inc(s["bias_in"], 16)
                    pool.wait_ge(s["bias_in"], 16 * (n + 1))
                    step(nc.gpsimd.memset(bias[0:L, n % 2, 0:L], MASKED))
                    if t >= 4:
                        step(nc.gpsimd.memset(bias[0:L, n % 2, w - L:w], MASKED))
                        step(nc.gpsimd.memset(bias[L:P, n % 2, P:w], MASKED))
                    pool.sem_inc(s["bias_ready"], 1)
            pool.wait_ge(s["o_lo"], 8)
            nc.gpsimd.memset(x_zero[:, :], 0.0).then_inc(s["zeroed"], 1)
            pool.wait_ge(s["w_split"], UNITS * G_ALL)
            pool.dma_start(gain_out, norm_final.to_broadcast([P, D])).then_inc(s["gout_in"], 16)

        @block.scalar
        def _(act):
            def copy(dst, src, scale=1.0):
                return nc.scalar.activation(dst, src, ACT.Copy, scale=scale)

            def hi(slot, landed, dst, used):
                act.wait_ge(w_landed[slot], 16 * landed)
                if used is not None:
                    act.wait_ge(s["w_used"], used)
                copy(dst, w_raw[:, slot, 0:dst.shape[-1]]).then_inc(s["w_hi_done"], 1)

            def hi_in(n):
                hi(n % RAW, n // RAW + 1, in_slot(w_hi, n), n - SPL_IN + 1 if n >= SPL_IN else None)

            def hi_next(g, u, last=False):
                g, u = (g, u + 1) if u + 1 < UNITS else (g + 1, 0)
                if not last:
                    hi(u % RAW, 2 * g + u // RAW + 1, rest_slot(w_hi, u), UNITS * g + u - SPL + 1)

            def square_sum(t, j, src, junk):
                nc.scalar.activation(junk, src, ACT.Square, accum_out=ssq[:, t, j:j + 1])
                act.drain()

            def root(k, tiles):
                act.sem_inc(s["ssq_act"], 1)
                act.wait_ge(s["ms_ready"], k + 1)
                nc.scalar.activation(rms[:, 4:4 + tiles], rms[:, 0:tiles], ACT.Sqrt).then_inc(s["rms_sqrt"], 1)

            def load_tables(func):
                nc.scalar.activation(tiny[:, :], ident[:, 0:1], func)
                act.drain()

            def set_squares(sidx, nb):
                for t in range(TT):
                    act.wait_ge(s["bank_evac"], 4 * sidx + t + 1)
                    square_sum(t, nb, h[:, t, nb * 512:(nb + 1) * 512], relu_t[:, t % 2, :])

            def normed_hi(k, kt, b, gidx, dst, n):
                act.wait_ge(s["tr_mm"], KT * k + kt + 1)
                copy(dst[:, kt, :], ps[:, b, 0:n], scale=gain[:, gidx, kt:kt + 1]).then_inc(s["norm_hi"], 1)

            def norm(k, gidx, dst, n):
                root(k, TT)
                for kt in range(KT):
                    normed_hi(k, kt, kt % 8, gidx, dst, n)

            act.wait_ge(s["zeroed"], 1)
            load_tables(ACT.Sqrt)
            for t in range(TT):
                act.wait_ge(x_in[t], 16)
                square_sum(t, 0, x_mix[:, t, 0:D // 2], ps[:, 0:2, :].rearrange("p a b -> p (a b)"))
            act.wait_ge(s["gain_in"], 16)
            norm(0, 0, act_hi, SEQ)
            for n in range(SPL_IN - 1):
                hi_in(n)

            mem_hi = mid_hi[:, :, :].rearrange("p a (b n) -> p (a b) n", n=N_MEM)

            def position(p, g):
                (q, elem), _, (f, fin) = stages(g)
                par = q % 2
                if g == G_IN - 1 and p == 8:
                    act.wait_ge(s["mem_in"], 32)
                    for t in range(2):
                        square_sum(t, 0, memx[:, t, 0:D // 2], mid_hi[:, 0:2, :].rearrange("p a b -> p (a b)"))
                    root(1, 2)
                for kt in mem_tiles(p, g):
                    normed_hi(1, kt, mem_bank(kt), 2, mem_hi, N_MEM)
                if p == 0 and elem:
                    act.wait_ge(s["small_prm"], q + 1)
                    act.wait_ge(s["zw_mm"], q + 1)
                    nc.scalar.activation(sg[:, :], bank(4), ACT.Tanh, scale=0.5,
                                         bias=col(prm2, HALF_W0)).then_inc(s["zw_ev"], 1)
                    act.wait_ge(s["za_mm"], q + 1)
                    nc.scalar.activation(aa[:, :], bank(5), ACT.Tanh, scale=0.5,
                                         bias=col(prm2, HALF_A0)).then_inc(s["za_ev"], 1)
                if p == 2 and elem:
                    act.wait_ge(s["shifted"], q + 1)
                    nc.scalar.activation(pad[0][:, 1:1 + SEQ], kk_[:, :], ACT.Square,
                                         scale=col(prm, K_K)).then_inc(s["sq_k"], 1)
                if p == 3 and fin:
                    if f:
                        act.wait_ge(s["y_fin"], f)
                    act.wait_ge(s["yc_ready"], f + 1)
                    nc.scalar.activation(ysq[:, :], yc[:, :], ACT.Square).then_inc(s["ysq_ready"], 1)
                if p == 3 and elem:
                    act.wait_ge(s["vtok_mm"], q + 1)
                    copy(v_tok[par][:, :], bank(3)).then_inc(s["vtok_ev"], 1)
                if p == 4 and elem:
                    act.wait_ge(s["cum_ready"], q + 1)
                    nc.scalar.activation(g_pad[:, :, 1:1 + L], chunks(cs), ACT.Exp, scale=-LOGW).then_inc(s["g_ready"], 1)
                    nc.scalar.activation(g_inv[:, :], cs[:, :], ACT.Exp, scale=LOGW).then_inc(s["g_ready"], 1)
                if p == 5 and fin:
                    act.wait_ge(s["gate_mm"], f + 1)
                    copy(gs[:, :], bank(5)).then_inc(s["gate_ev"], 1)
                if p == 6 and elem:
                    act.wait_ge(s["ss_max"], q + 1)
                    nc.scalar.activation(pad[1][:, 1:1 + SEQ], pad[1][:, 1:1 + SEQ], ACT.Sqrt).then_inc(s["ss_sqrt"], 1)
                if p == 7 and fin:
                    act.wait_ge(s["var_eps"], f + 1)
                    nc.scalar.activation(ysq[:, :], ysq[:, :], ACT.Sqrt).then_inc(s["var_sqrt"], 1)
                if p == 7 and elem:
                    load_tables(ACT.Exp)
                if p == 9 and elem:
                    act.wait_ge(s["ktok_mm"], q + 1)
                    copy(k_tok[par][:, :], bank(3)).then_inc(s["ktok_ev"], 1)
                if p == 13 and elem:
                    act.wait_ge(s["btok_mm"], q + 1)
                    copy(b_tok[par][:, :], bank(3)).then_inc(s["btok_ev"], 1)

            for g in range(G_IN):
                _, (c, chain), (f, fin) = stages(g)
                if fin:
                    act.wait_ge(s["y_mm"], f + 1)
                    copy(yb[:, :], bank(7)).then_inc(s["y_ev"], 1)
                for u in range(UNITS):
                    n = UNITS * g + u + SPL_IN - 1
                    if n < UNITS * G_IN:
                        hi_in(n)
                    if g == 1 and u == 0:
                        act.wait_ge(s["lora_shift"], 1)
                        nc.scalar.activation(lora[0:L, 0, :], lora[0:L, 0, :], ACT.Tanh).then_inc(s["lora_act"], 1)
                        nc.scalar.activation(lora[:, 1:3, :], lora[:, 1:3, :], ACT.Tanh, scale=0.5).then_inc(s["lora_act"], 1)
                    if chain:
                        act.wait_ge(s["z_mm"], NC * c + u + 1)
                        copy(z_s[:, :], ps[:, 6, 0:L]).then_inc(s["z_ev"], 1)
                    position(3 * u, g)
                    if chain:
                        act.wait_ge(s["u_mm"], NC * c + u + 1)
                        copy(u_s[:, :], ps[:, 6, L:2 * L]).then_inc(s["u_ev"], 1)
                    position(3 * u + 1, g)
                    position(3 * u + 2, g)
                if g == 0:
                    act.wait_ge(s["consts"], 1)
                elif g == 1:
                    act.wait_ge(s["lora_shift"], 1)
                elif qkv_block(g - 1)[0] is not None:
                    act.wait_ge(s["qkv_stored"], 48 * (qkv_block(g - 1)[1] + 1))
                else:
                    act.wait_ge(s["bon_ev"], g - G_PAIR)
                b, _ = qkv_block(g)
                act.wait_ge(s["w_used"], UNITS * (g + 1))
                for m in range(3):
                    is_q = b is not None and (3 * b + m < 4 or A_TILES <= 3 * b + m < A_TILES + 4)
                    copy(pad[m][:, 1:1 + SEQ], bank(m), scale=0.125 if is_q else 1.0).then_inc(s["in_evac"], 1)

            hi(0, UNITS * G_IN // RAW + 1, rest_slot(w_hi, 0), UNITS * G_IN)
            def att_step(st):
                n = st - 2
                if 0 <= n < N_UNITS_ATT:
                    keys = unit_of(n)[5]
                    act.wait_ge(s["pT_mm"], n + 1)
                    if n >= 2:
                        act.wait_ge(s["o_mm"], n - 1)
                    copy(att_pT[:, n % 2, 0:keys], ps[:, 6, 0:keys]).then_inc(s["pT_ev"], 1)
                n = st - 3
                if n >= 0 and n % 8 == 7:
                    t = n // 8
                    act.wait_ge(s["o_mm"], n + 1)
                    copy(act_hi[:, t if t < 4 else t + 8, :], bank(7)).then_inc(s["o_hi"], 1)
                n = st
                if n < N_UNITS_ATT:
                    kind, t, half, i, key0, keys = unit_of(n)
                    act.wait_ge(s["sc_neg"], n + 1)
                    if kind == "C":
                        head = (t - 4) + 4 * half
                        nc.scalar.activation(att_c[:, n % 4, 3:4], sink[:, head:head + 1], ACT.Exp,
                                             bias=att_c[:, n % 4, 1:2])
                    nc.scalar.activation(att_p[:, n % 4, 0:keys], att_p[:, n % 4, 0:keys], ACT.Exp,
                                         bias=att_c[:, n % 4, 1:2],
                                         accum_out=att_c[:, n % 4, 2:3]).then_inc(s["p_exp"], 1)

            act.wait_ge(s["sink_in"], 16)
            for g in range(G_XK, G_XQ):
                for u in range(UNITS):
                    v = UNITS * (g - G_XK) + u
                    hi_next(g, u)
                    if v < TT:
                        act.wait_ge(s["vt_mm"], v + 1)
                        copy(vt[:, v, :], ps[:, 6:8, :].rearrange("p a b -> p (a b)")[:, 0:640]).then_inc(s["vt_ev"], 1)
                    if 4 <= v < 4 + PAIRS:
                        act.wait_ge(s["y_landed"], 16 * PAIRS)
                        copy(act_hi[:, v, :], y_in[:, v - 4, :]).then_inc(s["y_hi"], 1)
                    for st in att_steps(v) if g < G_WA else ():
                        att_step(st)
                    if g >= G_WA and u % 4 == 0 and v > UNITS * (G_WA - G_XK):
                        nb = (v - UNITS * (G_WA - G_XK)) // 4 - 1
                        set_squares(S_WA + nb, nb)
            load_tables(ACT.Sqrt)
            set_squares(S_WA + 3, 3)
            norm(2, 1, act_hi, SEQ)
            load_tables(ACT.Exp)
            for u in range(UNITS):
                hi_next(G_XQ, u)
            for kb in range(2):
                act.wait_ge(s["xvt_mm"], kb + 1)
                copy(xv_tok[:, kb, :], bank(6)).then_inc(s["xvt_ev"], 1)
            for st in range(16 + 3):
                n = st
                if n < 16:
                    act.wait_ge(s["xs_neg"], n + 1)
                    if n >= 4:
                        act.wait_ge(s["xpT_mm"], n - 3)
                    nc.scalar.activation(x_p[:, n % 4, :], x_s[:, n % 2, :], ACT.Exp, bias=x_c[:, n % 4, 1:2],
                                         accum_out=x_c[:, n % 4, 2:3]).then_inc(s["xp_exp"], 1)
                n = st - 2
                if 0 <= n < 16:
                    act.wait_ge(s["xpT_mm"], n + 1)
                    if n >= 2:
                        act.wait_ge(s["xo_mm"], n - 1)
                    copy(x_pT[:, n % 2, :], ps[:, 2 + n % 2, 0:N_MEM]).then_inc(s["xpT_ev"], 1)
                n = st - 3
                if n >= 0 and n % 4 == 3:
                    act.wait_ge(s["xo_mm"], n + 1)
                    copy(mid_hi[:, n // 4, :], bank(4 + (n // 4) % 2)).then_inc(s["xo_hi"], 1)
            for u in range(UNITS):
                hi_next(G_XO, u)
                if u % 2 == 0 and u:
                    set_squares(S_XO + u // 2 - 1, u // 2 - 1)
            load_tables(ACT.Sqrt)
            set_squares(S_XO + 3, 3)
            norm(3, 3, act_hi, SEQ)

            def relu_tiles(c, j, tiles):
                for m in tiles:
                    r = m % 2
                    act.wait_ge(s["w_used"], UNITS * (G_MLP + 4 * c + j + 1))
                    if m >= 2:
                        act.wait_ge(s["bank_evac"], 4 * (S_MLP + 6 * c + j) + m - 1)
                    nc.scalar.activation(relu_t[:, r, :], bank(4 * ((S_MLP + j) % 2) + m), ACT.Relu).then_inc(s["relu_done"], 1)
                    act.wait_ge(s["relu_done"], 8 * c + 4 * j + m + 1)
                    nc.scalar.activation(mid_hi[:, 4 * j + m, :], relu_t[:, r, :], ACT.Square).then_inc(s["mid_hi_done"], 1)

            def mlp_chunk(c, last):
                g0 = G_MLP + 4 * c
                for b in range(4):
                    for u in range(UNITS):
                        hi_next(g0 + b, u, last and b == 3 and u == UNITS - 1)
                        if b in (1, 2) and u < 2:
                            relu_tiles(c, b - 1, (2 * u, 2 * u + 1))
                        if last and b >= 2 and u % 4 == 0 and 4 * (b - 2) + u:
                            nb = 2 * (b - 2) + u // 4 - 1
                            set_squares(S_MLP + 6 * c + 2 + nb, nb)

            with act.Fori(0, MLP_CHUNKS - 1) as c:
                mlp_chunk(c, False)
            mlp_chunk(MLP_CHUNKS - 1, True)
            load_tables(ACT.Sqrt)
            set_squares(S_MLP + 6 * MLP_CHUNKS - 1, 3)
            root(4, TT)

        @block.vector
        def _(dve):
            V = nc.vector

            def lo(n, slot, dst, high):
                dve.wait_ge(s["w_hi_done"], n + 1)
                V.tensor_tensor(dst, w_raw[:, slot, 0:dst.shape[-1]], high.bitcast(F32),
                                ALU.subtract).then_inc(s["w_split"], 1)

            def lo_in(n):
                lo(n, n % RAW, in_slot(w_lo, n), in_slot(w_hi, n))

            def lo_next(g, u, last=False):
                g, u = (g, u + 1) if u + 1 < UNITS else (g + 1, 0)
                if not last:
                    lo(UNITS * g + u, u % RAW, rest_slot(w_lo, u), rest_slot(w_hi, u))

            def square_sum(t, j, src, junk):
                V.tensor_tensor_reduce(out=junk, in0=src, in1=src, scale=1.0, scalar=0.0,
                                       op0=ALU.mult, op1=ALU.add, accum_out=ssq[:, t, j:j + 1])
                dve.drain()

            def inverse_rms(k, tiles, parts):
                dve.wait_ge(s["ssq_act"], k + 1)
                V.tensor_reduce(rms[:, 0:tiles], ssq[:, 0:tiles, 0:parts], axis=mybir.AxisListType.X, op=ALU.add)
                dve.drain()
                V.tensor_scalar(rms[:, 0:tiles], rms[:, 0:tiles], 1.0 / D, RMS_EPS, ALU.mult, ALU.add).then_inc(s["ms_ready"], 1)
                dve.wait_ge(s["rms_sqrt"], k + 1)
                V.reciprocal(rms[:, 0:tiles], rms[:, 4:4 + tiles])
                dve.drain()

            def diagonals(tiles):
                for t in range(tiles):
                    V.tensor_scalar(diag[:, t, :], ident[:, :], rms[:, t:t + 1], None, ALU.mult).then_inc(s["diag_ready"], 1)

            def normed_lo(k, kt, b, gidx, dst_hi, dst_lo, n):
                dve.wait_ge(s["norm_hi"], KT * k + kt + 1)
                V.scalar_tensor_tensor(dst_lo[:, kt, :], ps[:, b, 0:n], gain[:, gidx, kt:kt + 1],
                                       dst_hi[:, kt, :].bitcast(F32), ALU.mult, ALU.subtract).then_inc(s["norm_lo"], 1)

            def norm(k, parts, gidx, dst_hi, dst_lo, n):
                inverse_rms(k, TT, parts)
                diagonals(TT)
                for kt in range(KT):
                    normed_lo(k, kt, kt % 8, gidx, dst_hi, dst_lo, n)

            for t in range(TT):
                dve.wait_ge(x_in[t], 16)
                square_sum(t, 1, x_mix[:, t, D // 2:], ps[:, 4:6, :].rearrange("p a b -> p (a b)"))
            dve.wait_ge(s["gain_in"], 16)
            dve.wait_ge(s["zeroed"], 1)
            norm(0, 2, 0, act_hi, act_lo, SEQ)
            for n in range(SPL_IN - 1):
                lo_in(n)
            T1, T2 = pad[0][:, 1:1 + SEQ], pad[1][:, 1:1 + SEQ]
            ka_col, rk_col, kk_col = col(prm, K_A), col(prm, R_K), col(prm, K_K)

            def masked(dst, b, m):
                return V.tensor_tensor(chunks(dst), ps[:, b, :].rearrange("p (c t) -> p c t", c=NC),
                                       over_chunks(m), ALU.mult)

            mem_hi = mid_hi[:, :, :].rearrange("p a (b n) -> p (a b) n", n=N_MEM)
            mem_lo = mid_lo[:, :, :].rearrange("p a (b n) -> p (a b) n", n=N_MEM)

            def position(p, g):
                (q, elem), _, (f, fin) = stages(g)
                par = q % 2
                LV = len(LEVELS)
                if g == G_IN - 1 and p == 8:
                    dve.wait_ge(s["mem_in"], 32)
                    for t in range(2):
                        square_sum(t, 1, memx[:, t, D // 2:], mid_lo[:, 0:2, :].rearrange("p a b -> p (a b)"))
                    inverse_rms(1, 2, 2)
                    diagonals(2)
                for kt in mem_tiles(p, g):
                    normed_lo(1, kt, mem_bank(kt), 2, mem_hi, mem_lo, N_MEM)
                if p == 0 and elem:
                    dve.wait_ge(s["prm_in"], 16 * (q + 1))
                    V.tensor_scalar(prm2[:, 0:2], prm[:, W0:W0 + 2], 0.5, None, ALU.mult)
                    V.tensor_scalar(prm2[:, 2:3], ka_col, -1.0, 1.0, ALU.mult, ALU.add).then_inc(s["small_prm"], 1)
                    dve.wait_ge(s["in_evac"], 3 * (q + G_PAIR + 1))
                    for dst, src in zip((rr, kk_, vv), pad):
                        V.tensor_tensor(dst[:, :], src[:, 0:SEQ], src[:, 1:1 + SEQ], ALU.subtract)
                if p == 1 and elem:
                    dve.drain()
                    for i, (dst, src) in enumerate(zip((rr, kk_, vv), pad)):
                        last = V.scalar_tensor_tensor(dst[:, :], dst[:, :], col(prm, MU_R + i), src[:, 1:1 + SEQ],
                                                      ALU.mult, ALU.add)
                    last.then_inc(s["shifted"], 1)
                if p == 2 and fin:
                    dve.wait_ge(s["mean_mm"], f + 1)
                    if f:
                        dve.wait_ge(s["y_stored"], 16 * f)
                    V.tensor_tensor(yc[:, :], yb[:, :], bank(3), ALU.subtract).then_inc(s["yc_ready"], 1)
                if p == 2 and elem:
                    dve.wait_ge(s["zw_ev"], q + 1)
                    V.tensor_scalar(sg[:, :], sg[:, :], 0.5, 0.5, ALU.mult, ALU.add)
                    dve.wait_ge(s["za_ev"], q + 1)
                    V.tensor_scalar(aa[:, :], aa[:, :], 0.5, 0.5, ALU.mult, ALU.add)
                if p == 3 and elem:
                    dve.drain()
                    V.tensor_tensor_scan(cs[:, :], rm[:, :], sg[:, :], 0.0, ALU.mult, ALU.add).then_inc(s["cum_ready"], 1)
                    V.tensor_scalar(kp[:, :], aa[:, :], ka_col, prm2[:, 2:3], ALU.mult, ALU.add)
                if p == 5 and elem:
                    dve.wait_ge(s["ss_mm"], q + 1)
                    V.tensor_scalar(T2, bank(4), 1e-24, None, ALU.max).then_inc(s["ss_max"], 1)
                if p == 5 and fin:
                    dve.wait_ge(s["var_mm"], f + 1)
                    V.tensor_scalar(ysq[:, :], bank(3), GN_EPS, None, ALU.add).then_inc(s["var_eps"], 1)
                if p == 5 and elem:
                    dve.drain()
                    V.tensor_tensor(kp[:, :], kp[:, :], kk_[:, :], ALU.mult)
                if p == 6 and elem:
                    dve.drain()
                    V.scalar_tensor_tensor(T1, rr[:, :], rk_col, kp[:, :], ALU.mult, ALU.mult).then_inc(s["bon_in"], 1)
                if p == 6 and elem:
                    dve.wait_ge(s["g_ready"], 2 * (q + 1))
                    V.tensor_tensor(kk_dec[:, :], kp[:, :], g_inv[:, :], ALU.mult).then_inc(s["kt_ready"], 1)
                    V.tensor_tensor(chunks(rT[par]), chunks(rr), g_pad[:, :, 1:1 + L], ALU.mult)
                    V.tensor_copy(g_last[:, par, :], g_pad[:, :, L:L + 1].rearrange("p c o -> p (c o)"))
                if p == 7 and elem:
                    dve.wait_ge(s["ss_sqrt"], q + 1)
                    V.reciprocal(T2[:, 0:SEQ // 2], T2[:, 0:SEQ // 2])
                if p == 8 and elem:
                    V.reciprocal(T2[:, SEQ // 2:], T2[:, SEQ // 2:])
                    dve.drain()
                    V.scalar_tensor_tensor(kkn[:, :], kk_[:, :], kk_col, T2, ALU.mult, ALU.mult)
                if p == 8 and elem:
                    dve.drain()
                    V.scalar_tensor_tensor(chunks(aT[par]), chunks(kkn), -1.0, g_pad[:, :, 0:L],
                                           ALU.mult, ALU.mult).then_inc(s["ab_ready"], 1)
                if p == 9 and elem:
                    V.tensor_tensor(aa[:, :], aa[:, :], kkn[:, :], ALU.mult)
                if p == 10 and elem:
                    dve.drain()
                    V.tensor_tensor(aa[:, :], aa[:, :], g_inv[:, :], ALU.mult).then_inc(s["bt_ready"], 1)
                if p == 10 and elem:
                    dve.wait_ge(s["bon_mm"], q + 1)
                    if q >= 3:
                        dve.wait_ge(s["y_fin"], q - 2)
                    V.tensor_tensor(bonv[q % 3][:, :], bank(5), vv[:, :], ALU.mult).then_inc(s["bon_ev"], 1)
                if p == 11 and elem:
                    dve.wait_ge(s["mak_mm"], q + 1)
                    masked(makT[par], 4, mk_up[:, :]).then_inc(s["mak_ev"], 1)
                    dve.wait_ge(s["mrk_mm"], q + 1)
                    masked(mrkT[par], 5, mk_upi[:, :]).then_inc(s["mrk_ev"], 1)
                if p == 12 and elem:
                    dve.wait_ge(s["mab_mm"], q + 1)
                    masked(m_ab, 4, mk_lo[:, :]).then_inc(s["mab_ev"], 1)
                    dve.wait_ge(s["mabT_mm"], q + 1)
                    masked(m_abT, 5, mk_up[:, :]).then_inc(s["mabT_ev"], 1)
                if p == 13 and elem:
                    dve.drain()
                    V.tensor_tensor(chunks(inv), chunks(m_ab), over_chunks(mk_1[:, :]), ALU.mult)
                    V.tensor_tensor(chunks(invT[par]), chunks(m_abT), over_chunks(mk_1T[:, :]), ALU.mult)
                    dve.drain()
                    V.tensor_tensor(chunks(inv), chunks(inv), over_chunks(eye2[:, :]), ALU.add)
                    V.tensor_tensor(chunks(invT[par]), chunks(invT[par]), over_chunks(eye2[:, :]),
                                    ALU.add).then_inc(s["inv_init"], 1)
                if p == 13 and fin:
                    dve.wait_ge(s["var_sqrt"], f + 1)
                    V.reciprocal(ysq[:, :], ysq[:, :]).then_inc(s["rstd_ready"], 1)
                if p >= 14 and p % 2 == 0 and elem:
                    lv = (p - 14) // 2
                    dve.wait_ge(s["t_mm"], LV * q + lv + 1)
                    masked(t_lev, 4, mk_lev[:, lv, :]).then_inc(s["t_ev"], 1)
                    if lv == 0:
                        dve.wait_ge(s["mrb_mm"], q + 1)
                        masked(mrbT[par], 3, mk_upi[:, :]).then_inc(s["mrb_ev"], 1)
                if p >= 15 and p % 2 == 1 and elem:
                    lv = (p - 15) // 2
                    if lv < LV - 1:
                        dve.wait_ge(s["x_mm"], (LV - 1) * q + lv + 1)
                        V.tensor_tensor(inv[:, :], inv[:, :], bank(5), ALU.add).then_inc(s["x_ev"], 1)
                    dve.wait_ge(s["xT_mm"], LV * q + lv + 1)
                    V.tensor_tensor(invT[par][:, :], invT[par][:, :], bank(3), ALU.add).then_inc(s["xT_ev"], 1)

            for g in range(G_IN):
                _, (c, chain), _ = stages(g)
                for u in range(UNITS):
                    n = UNITS * g + u + SPL_IN - 1
                    if n < UNITS * G_IN:
                        lo_in(n)
                    if g == 1 and u == 0:
                        dve.wait_ge(s["in_evac"], 3)
                        dve.wait_ge(s["lmu_in"], 16)
                        for i in range(3):
                            V.tensor_tensor(lora[:, i, :], pad[i][:, 0:SEQ], pad[i][:, 1:1 + SEQ], ALU.subtract)
                        dve.drain()
                        for i in range(3):
                            last = V.scalar_tensor_tensor(lora[:, i, :], lora[:, i, :], col(lmu, i),
                                                          pad[i][:, 1:1 + SEQ], ALU.mult, ALU.add)
                        last.then_inc(s["lora_shift"], 1)
                    if g == 1 and u == 1:
                        dve.wait_ge(s["lora_act"], 2)
                        V.tensor_scalar(lora[:, 1:3, :], lora[:, 1:3, :], 0.5, 0.5, ALU.mult,
                                        ALU.add).then_inc(s["lora_act"], 1)
                    if chain and u:
                        dve.drain()
                        V.tensor_scalar(st_g[:, :], st_s[:, u % 2, :], g_last[:, c % 2, u:u + 1], None, ALU.mult)
                    for third in range(3):
                        if chain and third == 2 and u < NC - 1:
                            dve.wait_ge(s["s_mm"], (NC - 1) * c + u + 1)
                            dst, gl = st_s[:, (u + 1) % 2, :], g_last[:, c % 2, u:u + 1]
                            if u == 0:
                                V.tensor_scalar(dst, ps[:, 6, 2 * L:3 * L], gl, None, ALU.mult).then_inc(s["s_ev"], 1)
                            else:
                                dve.drain()
                                V.scalar_tensor_tensor(dst, ps[:, 6, 2 * L:3 * L], gl, st_g[:, :],
                                                       ALU.mult, ALU.add).then_inc(s["s_ev"], 1)
                        position(3 * u + third, g)

            lo(UNITS * G_IN, 0, rest_slot(w_lo, 0), rest_slot(w_hi, 0))

            def att_step(st):
                n = st - 1
                if 0 <= n < N_UNITS_ATT:
                    kind, keys = unit_of(n)[0], unit_of(n)[5]
                    dve.wait_ge(s["p_exp"], n + 1)
                    if kind == "C":
                        V.tensor_tensor(att_c[:, n % 4, 2:3], att_c[:, n % 4, 2:3], att_c[:, n % 4, 3:4], ALU.add)
                        dve.drain()
                    V.reciprocal(att_c[:, n % 4, 0:1], att_c[:, n % 4, 2:3])
                    dve.drain()
                    V.tensor_scalar(att_p[:, n % 4, 0:keys], att_p[:, n % 4, 0:keys], att_c[:, n % 4, 0:1], None,
                                    ALU.mult).then_inc(s["p_ready"], 1)
                n = st
                if n < N_UNITS_ATT:
                    kind, t, half, i, key0, keys = unit_of(n)
                    hd = n // 4
                    dve.wait_ge(s["sc_mm"], n + 1)
                    dve.wait_ge(s["bias_ready"], hd + 1)
                    if n >= 4:
                        dve.wait_ge(s["pT_mm"], n - 3)
                    V.tensor_tensor_reduce(out=att_p[:, n % 4, 0:keys], in0=ps[:, 4 + n % 2, 0:keys],
                                           in1=falling(bias[:, hd % 2, 0:keys]), scale=1.0, scalar=-3e38,
                                           op0=ALU.add, op1=ALU.max,
                                           accum_out=att_c[:, n % 4, 0:1]).then_inc(s["sc_max"], 1)
                    dve.wait_ge(s["sc_max"], n + 1)
                    if kind == "C":
                        head = (t - 4) + 4 * half
                        V.tensor_scalar(att_c[:, n % 4, 1:2], att_c[:, n % 4, 0:1], sink[:, head:head + 1], -1.0,
                                        ALU.max, ALU.mult).then_inc(s["sc_neg"], 1)
                    else:
                        V.tensor_scalar(att_c[:, n % 4, 1:2], att_c[:, n % 4, 0:1], -1.0, None,
                                        ALU.mult).then_inc(s["sc_neg"], 1)
                n = st - 3
                if n >= 0 and n % 8 == 7:
                    t = n // 8
                    mt = t if t < 4 else t + 8
                    dve.wait_ge(s["o_hi"], t + 1)
                    V.tensor_tensor(act_lo[:, mt, :], bank(7), act_hi[:, mt, :].bitcast(F32),
                                    ALU.subtract).then_inc(s["o_lo"], 1)

            def add_set(units, par, nb):
                dve.wait_ge(s["w_used"], units)
                for t in range(TT):
                    dst = h[:, t, nb * 512:(nb + 1) * 512]
                    V.tensor_tensor(dst, dst, bank(4 * par + t), ALU.add).then_inc(s["bank_evac"], 1)

            def copy_set(units, sidx, dst, n, scale=1.0):
                dve.wait_ge(s["w_used"], units)
                for m in range(4):
                    V.tensor_scalar(dst[:, m, :], ps[:, 4 * (sidx % 2) + m, 0:n], scale, None,
                                    ALU.mult).then_inc(s["bank_evac"], 1)

            dve.wait_ge(s["sink_in"], 16)
            for g in range(G_XK, G_XQ):
                for u in range(UNITS):
                    v = UNITS * (g - G_XK) + u
                    lo_next(g, u)
                    if 4 <= v < 4 + PAIRS:
                        dve.wait_ge(s["y_hi"], v - 3)
                        V.tensor_tensor(act_lo[:, v, :], y_in[:, v - 4, :], act_hi[:, v, :].bitcast(F32),
                                        ALU.subtract).then_inc(s["y_lo"], 1)
                    for st in att_steps(v) if g < G_WA else ():
                        att_step(st)
                    if g < G_WR and u == UNITS - 1:
                        copy_set(UNITS * (g + 1), 0, (xk_t, xv_t)[g - G_XK], N_MEM)
                    if g == G_WR and u == 3:
                        dve.wait_ge(s["h_in"], 16 * TT)
                    if g >= G_WR and u % 4 == 3:
                        nb = (v - UNITS * 2) // 4 % 4
                        add_set(UNITS * g + u + 1, nb % 2 if g >= G_WA else 0, nb)
            dve.drain()
            norm(2, 4, 1, act_hi, act_lo, SEQ)
            for u in range(UNITS):
                lo_next(G_XQ, u)
            copy_set(UNITS * (G_XQ + 1), S_XQ, xq_t, SEQ, X_SCALE)
            dve.wait_ge(s["zeroed"], 2)
            for st in range(16 + 3):
                n = st
                if n < 16:
                    dve.wait_ge(s["xs_mm"], n + 1)
                    if n >= 2:
                        dve.wait_ge(s["xp_exp"], n - 1)
                    V.tensor_tensor_reduce(out=x_s[:, n % 2, :], in0=ps[:, n % 2, 0:N_MEM], in1=x_zero[:, :],
                                           scale=1.0, scalar=-3e38, op0=ALU.add, op1=ALU.max,
                                           accum_out=x_c[:, n % 4, 0:1]).then_inc(s["xs_max"], 1)
                    dve.wait_ge(s["xs_max"], n + 1)
                    V.tensor_scalar(x_c[:, n % 4, 1:2], x_c[:, n % 4, 0:1], -1.0, None, ALU.mult).then_inc(s["xs_neg"], 1)
                n = st - 1
                if 0 <= n < 16:
                    dve.wait_ge(s["xp_exp"], n + 1)
                    V.reciprocal(x_c[:, n % 4, 0:1], x_c[:, n % 4, 2:3])
                    dve.drain()
                    V.tensor_scalar(x_p[:, n % 4, :], x_p[:, n % 4, :], x_c[:, n % 4, 0:1], None,
                                    ALU.mult).then_inc(s["xp_ready"], 1)
                n = st - 3
                if n >= 0 and n % 4 == 3:
                    dve.wait_ge(s["xo_hi"], n // 4 + 1)
                    V.tensor_tensor(mid_lo[:, n // 4, :], bank(4 + (n // 4) % 2), mid_hi[:, n // 4, :].bitcast(F32),
                                    ALU.subtract).then_inc(s["xo_lo"], 1)
            for u in range(UNITS):
                lo_next(G_XO, u)
                if u % 2:
                    add_set(UNITS * G_XO + u + 1, (S_XO + u // 2) % 2, u // 2)
            dve.drain()
            norm(3, 4, 3, act_hi, act_lo, SEQ)

            def square_tiles(c, j, tiles):
                for m in tiles:
                    r = m % 2
                    dve.wait_ge(s["relu_done"], 8 * c + 4 * j + m + 1)
                    V.scalar_tensor_tensor(sq_t[:, r, :], bank(4 * ((S_MLP + j) % 2) + m), 0.0, relu_t[:, r, :],
                                           ALU.max, ALU.mult).then_inc(s["bank_evac"], 1)
                    dve.wait_ge(s["mid_hi_done"], 8 * c + 4 * j + m + 1)
                    dve.wait_ge(s["bank_evac"], 4 * (S_MLP + 6 * c + j) + m + 1)
                    V.tensor_tensor(mid_lo[:, 4 * j + m, :], sq_t[:, r, :], mid_hi[:, 4 * j + m, :].bitcast(F32),
                                    ALU.subtract).then_inc(s["mid_done"], 1)

            def mlp_chunk(c, last):
                g0 = G_MLP + 4 * c
                for b in range(4):
                    for u in range(UNITS):
                        lo_next(g0 + b, u, last and b == 3 and u == UNITS - 1)
                        if b in (1, 2) and u < 2:
                            square_tiles(c, b - 1, (2 * u, 2 * u + 1))
                        if b >= 2 and u % 4 == 3:
                            nb = 2 * (b - 2) + u // 4
                            add_set(UNITS * (g0 + b) + u + 1, (S_MLP + nb) % 2, nb)

            with dve.Fori(0, MLP_CHUNKS - 1) as c:
                mlp_chunk(c, False)
            mlp_chunk(MLP_CHUNKS - 1, True)
            dve.drain()
            inverse_rms(4, TT, 4)
            dve.wait_ge(s["gout_in"], 16)
            for t in range(TT):
                V.scalar_tensor_tensor(h[:, t, :], h[:, t, :], rms[:, t:t + 1], gain_out,
                                       ALU.mult, ALU.mult).then_inc(s["out_ready"], 1)

        @block.tensor
        def _(pe):
            mm = nc.tensor.matmul

            def split_mm(dst, a_hi, a_lo, b_hi, b_lo, start, stop):
                mm(dst, a_hi, b_hi, start=start, stop=False)
                mm(dst, a_hi, b_lo, start=False, stop=False)
                return mm(dst, a_lo, b_hi, start=False, stop=stop)

            def turned(k, kt, b, src, tiles):
                for t in range(tiles):
                    last = mm(ps[:, b, t * P:(t + 1) * P], src[:, t, kt * P:(kt + 1) * P], diag[:, t, :],
                              start=True, stop=True)
                last.then_inc(s["tr_mm"], 1)

            def norm(k, src, tiles):
                pe.wait_ge(s["diag_ready"], [0, TT, TT + 2, 2 * TT + 2][k] + tiles)
                for kt in range(KT):
                    if kt >= 8:
                        pe.wait_ge(s["norm_lo"], KT * k + kt - 7)
                    turned(k, kt, kt % 8, src, tiles)
                pe.wait_ge(s["norm_lo"], KT * (k + 1))

            def both(dst, lhsT, rhs, start, stop):
                for hf in HALF:
                    last = mm(dst[hf], lhsT[hf], rhs[hf], start=start, stop=stop)
                return last

            def grams(b, lhsT, rhs):
                for c in range(NC):
                    last = both(ps[:, b, part(c)], lhsT[:, part(c)], rhs[:, part(c)], True, True)
                return last

            def to_tokens(b, src):
                for c in range(NC):
                    last = both(ps[:, b, part(c)], src[:, part(c)], eye2, True, True)
                return last

            norm(0, x_mix, TT)
            T1 = pad[0][:, 1:1 + SEQ]
            LV = len(LEVELS)

            def position(p, g):
                (q, elem), _, (f, fin) = stages(g)
                par = q % 2
                for kt in mem_tiles(p, g):
                    if kt == 0:
                        pe.wait_ge(s["diag_ready"], TT + 2)
                        pe.wait_ge(s["gate_ev"], PAIRS)
                        pe.wait_ge(s["var_eps"], PAIRS)
                    if kt >= 5:
                        pe.wait_ge(s["norm_lo"], KT + kt - 4)
                    turned(1, kt, mem_bank(kt), memx, 2)
                if p == 0 and elem:
                    pe.wait_ge(s["prm_in"], 16 * (q + 1))
                    pe.wait_ge(s["lora_act"], 3)
                    if q:
                        pe.wait_ge(s["t_ev"], LV * q)
                        pe.wait_ge(s["x_ev"], (LV - 1) * q)
                    mm(bank(4), prm[0:L, N_PRM:], lora[0:L, 0, :], start=True, stop=True).then_inc(s["zw_mm"], 1)
                    mm(bank(5), prm[L:P, N_PRM:], lora[L:P, 0, :], start=True, stop=True).then_inc(s["za_mm"], 1)
                if p == 1 and fin:
                    pe.wait_ge(s["y_ev"], f + 1)
                    pe.wait_ge(s["xT_ev"], LV * min(q, PAIRS))
                    mm(bank(3), mean2[:, :], yb[:, :], start=True, stop=True).then_inc(s["mean_mm"], 1)
                if p == 3 and elem:
                    pe.wait_ge(s["shifted"], q + 1)
                    if fin:
                        pe.wait_ge(s["yc_ready"], f + 1)
                    elif q:
                        pe.wait_ge(s["xT_ev"], LV * q)
                    to_tokens(3, vv).then_inc(s["vtok_mm"], 1)
                if p == 4 and elem:
                    pe.wait_ge(s["sq_k"], q + 1)
                    pe.wait_ge(s["zw_ev"], q + 1)
                    mm(bank(4), ones2[:, :], T1, start=True, stop=True).then_inc(s["ss_mm"], 1)
                if p == 5 and fin:
                    pe.wait_ge(s["ysq_ready"], f + 1)
                    if elem:
                        pe.wait_ge(s["vtok_ev"], q + 1)
                        pe.wait_ge(s["za_ev"], q + 1)
                    mm(bank(3), mean2[:, :], ysq[:, :], start=True, stop=True).then_inc(s["var_mm"], 1)
                    pe.wait_ge(s["fprm_in"], 32 * (f + 1))
                    mm(bank(5), fprm[:, 2:2 + P], lora[:, 1, :], start=True, stop=False)
                    mm(bank(5), gup2[96:P, :], lora[96:P, 2, :], start=False, stop=True).then_inc(s["gate_mm"], 1)
                if p == 8 and elem:
                    pe.wait_ge(s["bon_in"], q + 1)
                    if fin:
                        pe.wait_ge(s["gate_ev"], f + 1)
                    pe.wait_ge(s["za_ev"], q + 1)
                    mm(bank(5), ones2[:, :], T1, start=True, stop=True).then_inc(s["bon_mm"], 1)
                if p == 9 and elem:
                    pe.wait_ge(s["kt_ready"], q + 1)
                    pe.wait_ge(s["vtok_ev"], q + 1)
                    if fin:
                        pe.wait_ge(s["var_eps"], f + 1)
                    to_tokens(3, kk_dec).then_inc(s["ktok_mm"], 1)
                if p == 10 and elem:
                    pe.wait_ge(s["ab_ready"], q + 1)
                    pe.wait_ge(s["ss_max"], q + 1)
                    grams(4, kk_dec, aT[par]).then_inc(s["mak_mm"], 1)
                if p == 11 and elem:
                    pe.wait_ge(s["bon_ev"], q + 1)
                    grams(5, kk_dec, rT[par]).then_inc(s["mrk_mm"], 1)
                if p == 12 and elem:
                    pe.wait_ge(s["bt_ready"], q + 1)
                    pe.wait_ge(s["mak_ev"], q + 1)
                    grams(4, aT[par], aa).then_inc(s["mab_mm"], 1)
                    pe.wait_ge(s["mrk_ev"], q + 1)
                    grams(5, aa, aT[par]).then_inc(s["mabT_mm"], 1)
                if p == 13 and elem:
                    pe.wait_ge(s["ktok_ev"], q + 1)
                    to_tokens(3, aa).then_inc(s["btok_mm"], 1)
                if p >= 14 and p % 2 == 0 and elem:
                    lv = (p - 14) // 2
                    if lv == 0:
                        pe.wait_ge(s["btok_ev"], q + 1)
                        grams(3, aa, rT[par]).then_inc(s["mrb_mm"], 1)
                        pe.wait_ge(s["inv_init"], q + 1)
                    else:
                        pe.wait_ge(s["x_ev"], (LV - 1) * q + lv)
                    grams(4, m_abT, inv).then_inc(s["t_mm"], 1)
                if p >= 15 and p % 2 == 1 and elem:
                    lv = (p - 15) // 2
                    pe.wait_ge(s["t_ev"], LV * q + lv + 1)
                    if lv:
                        pe.wait_ge(s["xT_ev"], LV * q + lv)
                    if lv < LV - 1:
                        grams(5, invT[par], t_lev).then_inc(s["x_mm"], 1)
                    pe.wait_ge(s["mrb_ev"], q + 1)
                    grams(3, t_lev, invT[par]).then_inc(s["xT_mm"], 1)

            def chain_z(c, u):
                par = c % 2
                dst = ps[:, 6, 0:L]
                if u:
                    pe.wait_ge(s["s_ev"], (NC - 1) * c + u)
                last = both(dst, makT[par][:, part(u)], v_tok[par][:, part(u)], True, u == 0)
                if u:
                    last = both(dst, aT[par][:, part(u)], st_s[:, u % 2, :], False, True)
                last.then_inc(s["z_mm"], 1)

            def chain_u(c, u):
                par = c % 2
                if u == 0:
                    pe.wait_ge(s["xT_ev"], LV * (c + 1))
                pe.wait_ge(s["z_ev"], NC * c + u + 1)
                both(ps[:, 6, L:2 * L], invT[par][:, part(u)], z_s, True, True).then_inc(s["u_mm"], 1)

            def chain_sy(c, u):
                par = c % 2
                pe.wait_ge(s["u_ev"], NC * c + u + 1)
                if u < NC - 1:
                    both(ps[:, 6, 2 * L:3 * L], b_tok[par][:, part(u)], u_s, True, False)
                    both(ps[:, 6, 2 * L:3 * L], k_tok[par][:, part(u)], v_tok[par][:, part(u)], False, True).then_inc(s["s_mm"], 1)
                if u == 0 and c:
                    pe.wait_ge(s["y_ev"], c)
                dst = ps[:, 7, part(u)]
                both(dst, u_s, mrbT[par][:, part(u)], True, False)
                last = both(dst, v_tok[par][:, part(u)], mrkT[par][:, part(u)], False, u == 0)
                if u:
                    last = both(dst, st_s[:, u % 2, :], rT[par][:, part(u)], False, True)
                if u == NC - 1:
                    last.then_inc(s["y_mm"], 1)

            for g in range(G_IN):
                _, (c, chain), _ = stages(g)
                cols = (0, P, 160) if g == 0 else (0, P, 2 * P)
                for u in range(UNITS):
                    pe.wait_ge(s["w_split"], UNITS * g + u + 1)
                    wh = in_slot(w_hi, UNITS * g + u).rearrange("p (c n) -> p c n", c=2)
                    wl = in_slot(w_lo, UNITS * g + u).rearrange("p (c n) -> p c n", c=2)
                    combos = [(k, m) for k in range(2) for m in range(3)]
                    for third in range(3):
                        if chain and third == 0:
                            chain_z(c, u)
                        if chain and third == 1:
                            chain_u(c, u)
                        if chain and third == 2:
                            chain_sy(c, u)
                        position(3 * u + third, g)
                        for k, m in combos[2 * third:2 * third + 2]:
                            kt = 2 * u + k
                            if kt == 0 and g:
                                pe.wait_ge(s["in_evac"], 3 * (g - 1) + m + 1)
                            cs_ = slice(cols[m], cols[m] + P)
                            last = split_mm(bank(m), wh[:, k, cs_], wl[:, k, cs_], act_hi[:, kt, :], act_lo[:, kt, :],
                                            kt == 0, kt == KT - 1)
                    last.then_inc(s["w_used"], 1)

            v_src = [att_pT[:, 0, :]] + [pad[i][:, 1:1 + SEQ] for i in range(3)] + [att_pT[:, 1, :]]

            def v_tiles(kb):
                if kb:
                    pe.wait_ge(s["vt_ev"], kb)
                for ft in range(5):
                    dst = ps[:, 6:8, :].rearrange("p a b -> p (a b)")[:, ft * P:(ft + 1) * P]
                    last = nc.tensor.transpose(dst, v_src[ft][:, kb * P:(kb + 1) * P], ident[:, :])
                last.then_inc(s["vt_mm"], 1)

            def att_step(st):
                n = st
                if n < N_UNITS_ATT:
                    kind, t, half, i, key0, keys = unit_of(n)
                    if n == 0:
                        pe.wait_ge(s["vt_ev"], TT)
                    if n % 8 == 0:
                        pe.wait_ge(s["qk_in"], 32 * (t + 1))
                    if n >= 2:
                        pe.wait_ge(s["sc_max"], n - 1)
                    hf = HALF[half]
                    mm(ps[:, 4 + n % 2, 0:keys], qk[hf, t % 2, 0, i * P:(i + 1) * P], qk[hf, t % 2, 1, key0:key0 + keys],
                       start=True, stop=True).then_inc(s["sc_mm"], 1)
                n = st - 2
                if 0 <= n < N_UNITS_ATT:
                    keys = unit_of(n)[5]
                    pe.wait_ge(s["p_ready"], n + 1)
                    if n:
                        pe.wait_ge(s["pT_ev"], n)
                    for b in range(keys // P):
                        last = nc.tensor.transpose(ps[:, 6, b * P:(b + 1) * P],
                                                   att_p[:, n % 4, b * P:(b + 1) * P], ident[:, :])
                    last.then_inc(s["pT_mm"], 1)
                n = st - 3
                if n >= 0:
                    kind, t, half, i, key0, keys = unit_of(n)
                    pe.wait_ge(s["pT_ev"], n + 1)
                    if n % 8 == 0 and t:
                        pe.wait_ge(s["o_lo"], t)
                    v0 = t * P + half * L if kind == "A" else 512 + half * L
                    nb = keys // P
                    for b in range(nb):
                        last = mm(ps[HALF[half], 7, i * P:(i + 1) * P], vt[:, key0 // P + b, v0:v0 + L],
                                  att_pT[:, n % 2, b * P:(b + 1) * P], start=b == 0, stop=b == nb - 1)
                    last.then_inc(s["o_mm"], 1)

            def rest_unit(n, u, stationary, a_hi, a_lo, kts, cols, par, first, last_kt, reused, side=None):
                pe.wait_ge(s["w_split"], n + 1)
                wh = rest_slot(w_hi, u).rearrange("p (c n) -> p c n", c=2)
                wl = rest_slot(w_lo, u).rearrange("p (c n) -> p c n", c=2)
                for k, kt in enumerate(kts):
                    for m in range(4):
                        if side is not None:
                            side(4 * k + m)
                        mp = slice(m * P, (m + 1) * P)
                        if kt == first and reused is not None:
                            pe.wait_ge(s["bank_evac"], 4 * reused + m + 1)
                        start, stop = kt == first, kt == last_kt
                        if stationary == "w":
                            last = split_mm(ps[:, 4 * par + m, 0:cols], wh[:, k, mp], wl[:, k, mp],
                                            a_hi[:, kt, :], a_lo[:, kt, :], start, stop)
                        else:
                            last = split_mm(bank(4 * par + m), a_hi[:, kt, mp], a_lo[:, kt, mp], wh[:, k, :], wl[:, k, :],
                                            start, stop)
                last.then_inc(s["w_used"], 1)

            pe.wait_ge(s["norm_lo"], 2 * KT)
            pe.wait_ge(s["v_in"], 32)
            mem_hi = mid_hi[:, :, :].rearrange("p a (b n) -> p (a b) n", n=N_MEM)
            mem_lo = mid_lo[:, :, :].rearrange("p a (b n) -> p (a b) n", n=N_MEM)
            for g in range(G_XK, G_XQ):
                for u in range(UNITS):
                    v = UNITS * (g - G_XK) + u
                    todo = att_steps(v) if g < G_WA else []

                    def side(i):
                        if v == 0 and i < 3:
                            pe.wait_ge(s["in_evac"], 3 * (G_IN - 1) + i + 1)
                        if v < TT and i == 4:
                            v_tiles(v)
                        for j, st in enumerate(todo):
                            if i == (8 * j + 4) // len(todo):
                                att_step(st)

                    n = UNITS * g + u
                    if g < G_WR:
                        rest_unit(n, u, "w", mem_hi, mem_lo, (2 * u, 2 * u + 1), N_MEM, 0, 0, KT - 1,
                                  S_XK if g == G_XV else None, side)
                        continue
                    kts = RWKV_KT if g < G_WA else ATT_KT
                    nb = (v - 2 * UNITS) // 4 % 4
                    sidx = (S_WR if g < G_WA else S_WA) + nb
                    if g == G_WR and u == 0:
                        pe.wait_ge(s["y_lo"], PAIRS)
                    if g == G_WA and u == 0:
                        pe.wait_ge(s["o_lo"], 8)
                    reused = sidx - 1 if sidx <= S_WA else None if sidx == S_WA + 1 else sidx - 2
                    k0 = 2 * (u % 4)
                    rest_unit(n, u, "a", act_hi, act_lo, kts[k0:k0 + 2], 512, nb % 2 if g >= G_WA else 0, kts[0], kts[-1],
                              reused, side)
            norm(2, h, TT)
            for u in range(UNITS):
                rest_unit(UNITS * G_XQ + u, u, "w", act_hi, act_lo, (2 * u, 2 * u + 1), SEQ, S_XQ % 2, 0, KT - 1, S_XQ - 2)
            for kb in range(2):
                if kb:
                    pe.wait_ge(s["xvt_ev"], kb)
                for t in range(4):
                    last = nc.tensor.transpose(ps[:, 6, t * P:(t + 1) * P], xv_t[:, t, kb * P:(kb + 1) * P], ident[:, :])
                last.then_inc(s["xvt_mm"], 1)
            pe.wait_ge(s["xvt_ev"], 2)
            pe.wait_ge(s["bank_evac"], 4 * S_XO)
            for st in range(16 + 3):
                n = st
                if n < 16:
                    if n >= 2:
                        pe.wait_ge(s["xs_max"], n - 1)
                    mm(ps[:, n % 2, 0:N_MEM], xq_t[:, n // 4, (n % 4) * P:(n % 4 + 1) * P], xk_t[:, n // 4, :],
                       start=True, stop=True).then_inc(s["xs_mm"], 1)
                n = st - 2
                if 0 <= n < 16:
                    pe.wait_ge(s["xp_ready"], n + 1)
                    if n >= 2:
                        pe.wait_ge(s["xpT_ev"], n - 1)
                    for b in range(2):
                        last = nc.tensor.transpose(ps[:, 2 + n % 2, b * P:(b + 1) * P], x_p[:, n % 4, b * P:(b + 1) * P],
                                                   ident[:, :])
                    last.then_inc(s["xpT_mm"], 1)
                n = st - 3
                if n >= 0:
                    t, i = n // 4, n % 4
                    pe.wait_ge(s["xpT_ev"], n + 1)
                    if i == 0 and t >= 2:
                        pe.wait_ge(s["xo_lo"], t - 1)
                    for b in range(2):
                        last = mm(ps[:, 4 + t % 2, i * P:(i + 1) * P], xv_tok[:, b, t * P:(t + 1) * P],
                                  x_pT[:, n % 2, b * P:(b + 1) * P], start=b == 0, stop=b == 1)
                    last.then_inc(s["xo_mm"], 1)
            pe.wait_ge(s["xo_lo"], 4)
            for u in range(UNITS):
                nb, k0 = u // 2, 2 * (u % 2)
                rest_unit(UNITS * G_XO + u, u, "a", mid_hi, mid_lo, (k0, k0 + 1), 512, (S_XO + nb) % 2, 0, 3, S_XO + nb - 2)
            norm(3, h, TT)

            def mlp_chunk(c):
                g0 = G_MLP + 4 * c
                for b in range(2):
                    for u in range(UNITS):
                        rest_unit(UNITS * (g0 + b) + u, u, "w", act_hi, act_lo, (2 * u, 2 * u + 1), SEQ,
                                  (S_MLP + b) % 2, 0, KT - 1, S_MLP + 6 * c + b - 2)
                for v in range(2 * UNITS):
                    nb, k0 = v // 4, 2 * (v % 4)
                    if nb == 0:
                        pe.wait_ge(s["mid_done"], FT * c + k0 + 2)
                    rest_unit(UNITS * (g0 + 2) + v, v % UNITS, "a", mid_hi, mid_lo, (k0, k0 + 1), 512,
                              (S_MLP + nb) % 2, 0, FT - 1, S_MLP + 6 * c + nb)

            with pe.Fori(0, MLP_CHUNKS) as c:
                mlp_chunk(c)


def kernel(x, mem, norm_mix, w_in, w_vres_down, w_out, a_rel_bias, rwkv_mu, rwkv_mu_vres, rwkv_w0, rwkv_w_up, rwkv_a0,
           rwkv_a_up, rwkv_v0, rwkv_v_up, rwkv_g_up, rwkv_k_k, rwkv_k_a, rwkv_r_k, rwkv_ln_w, rwkv_ln_b, c_sinks,
           t5_bias, norm_x, norm_mem, x_wq, x_wk, x_wv, x_wo, norm_mlp, mlp_w1, mlp_w2, norm_final):
    import math

    import concourse.bacc as _bacc
    from concourse.bass_utils import run_bass_kernel_spmd as _run

    def units(w):
        rows, cols = w.shape
        return w.reshape(rows // (2 * P), 2, P, cols).transpose(0, 2, 1, 3).reshape(rows // (2 * P), P, 2 * cols)

    def by_columns(w, n):
        return [units(w[:, j:j + n]) for j in range(0, w.shape[1], n)]

    arr = np.asarray
    wi, wo = arr(w_in)[0], arr(w_out)[0]
    b_off, b_w = 1536, 1024
    c_off = b_off + 3 * b_w + LORA_W
    pair_of = [np.concatenate([wi[:, b_off + j * b_w + p * P:b_off + j * b_w + (p + 1) * P] for j in range(3)], axis=1)
               for p in range(PAIRS)]
    q_cols = np.concatenate([np.arange(hd * L, (hd + 1) * L) for t in range(4) for hd in (t, 4 + t)])
    w_c = np.concatenate([wi[:, c_off + q_cols], wi[:, c_off + 512:c_off + 768]], axis=1)
    w_lora = units(wi[:, b_off + 3 * b_w:c_off])
    w_pairs = np.concatenate(by_columns(w_c, PAIR_W) + [units(w) for w in pair_of] + by_columns(wi[:, 0:b_off], PAIR_W))
    wo_p = np.concatenate([wo[0:1536], wo[1536 + q_cols]])
    w1, w2 = arr(mlp_w1)[0], arr(mlp_w2)[0]
    mlp = []
    for c in range(MLP_CHUNKS):
        f = slice(c * FT * P, (c + 1) * FT * P)
        mlp += by_columns(w1[:, f], REST_W) + by_columns(w2[f], REST_W)
    w_rest = np.concatenate([units(arr(x_wk)[0]), units(arr(x_wv)[0])] + by_columns(wo_p[512:1536], REST_W)
                            + by_columns(np.concatenate([wo_p[0:512], wo_p[1536:]]), REST_W) + [units(arr(x_wq)[0])]
                            + by_columns(arr(x_wo)[0], REST_W) + mlp)

    def feature(v):
        return arr(v).reshape(-1, P).T

    mu = arr(rwkv_mu)[0]
    vecs = [mu[0:1024], mu[1024:2048], mu[2048:3072], arr(rwkv_w0)[0], arr(rwkv_a0)[0], arr(rwkv_k_k)[0],
            arr(rwkv_k_a)[0], arr(rwkv_r_k)[0].reshape(-1)]
    prm = np.stack([v.reshape(PAIRS, P) for v in vecs], axis=2)
    wa_up = np.concatenate([arr(rwkv_w_up)[0], arr(rwkv_a_up)[0]], axis=0).reshape(P, PAIRS, P).transpose(1, 0, 2)
    g_up = arr(rwkv_g_up)[0].reshape(160, PAIRS, P).transpose(1, 0, 2)
    fin = np.stack([arr(rwkv_ln_w)[0].reshape(PAIRS, P), arr(rwkv_ln_b)[0].reshape(PAIRS, P)], axis=2)
    mul = mu[3072:]
    rel_a = np.clip(np.arange(A_KEYS + P - 1) - (P - 1), -128, 128) + 128
    dist = (P - 1) - np.arange(C_KEYS + P - 1)
    near = np.abs(dist)
    large = 8 + (np.log(np.maximum(near, 1) / 8) / math.log(128 / 8) * 8).astype(np.int32)
    bucket = (dist > 0) * 16 + np.where(near < 8, near, np.minimum(large, 15))
    data = {
        "x": arr(x)[0], "mem": arr(mem)[0],
        "gains": np.stack([feature(arr(v)[0]) for v in (norm_mix, norm_x, norm_mem, norm_mlp)], axis=1),
        "w_lora": w_lora, "w_pairs": w_pairs, "w_rest": w_rest,
        "pair_prm": np.concatenate([prm, wa_up], axis=2),
        "fin_prm": np.concatenate([fin, g_up[:, 0:P]], axis=2), "gup_tail": g_up[:, P:],
        "lora_mu": np.stack([mul[0:P], mul[P:2 * P], mul[160:288]], axis=1),
        "a_line": arr(a_rel_bias)[0][rel_a].T, "c_line": arr(t5_bias)[bucket].T,
        "sinks": arr(c_sinks), "norm_final": arr(norm_final).reshape(1, D),
    }
    data = {f"in_{k}": np.ascontiguousarray(v) for k, v in data.items()}
    nc = _bacc.Bacc("TRN2", target_bir_lowering=False, num_devices=1)
    args = [nc.dram_tensor(k, v.shape, mybir.dt.from_np(v.dtype), kind="ExternalInput").ap() for k, v in data.items()]
    out = nc.dram_tensor("out_0", (SEQ, D), F32, kind="ExternalOutput").ap()
    hybrid_layer(nc, *args, out)
    r = _run(nc, [data], core_ids=[0])
    return r.results[0]["out_0"].reshape(1, SEQ, D)
```
